# Optimizing a Trainium2 kernel written in Bass

```python
import jax, jax.numpy as jnp
from jax import lax
import numpy as np

D_MODEL = 1024
BATCH = 1
SEQ = 512
DEPTH = 1

N_HEADS = 8
QK_NOPE_DIM = 64
QK_ROPE_DIM = 32
V_HEAD_DIM = 64
Q_LORA_RANK = 256
KV_LORA_RANK = 128
ATTN_WIDTH = N_HEADS * V_HEAD_DIM
CONV_WIDTH = 512
CONV_K = 3
N_BRANCH = 2
BRANCH_WIDTH = 512
D_FF = 2816
N_SUB = 3
ROPE_THETA = 10000.0
Q_BLOCK = 128
EPS = 1e-6
IN_COLS = Q_LORA_RANK + KV_LORA_RANK + QK_ROPE_DIM + 3 * CONV_WIDTH + N_BRANCH * D_MODEL


def rms_norm(x, w):
    xf = x.astype(jnp.float32)
    y = xf * lax.rsqrt(jnp.mean(xf * xf, axis=-1, keepdims=True) + EPS)
    return (y * w.astype(jnp.float32)).astype(x.dtype)

def modulate(x, w, shift, scale):
    return rms_norm(x, w) * (1 + scale[:, None, :]) + shift[:, None, :]

def swiglu(h, w13, w2):
    gu = jnp.einsum('bsd,df->bsf', h, w13)
    g, u = jnp.split(gu, 2, axis=-1)
    return jnp.einsum('bsf,fd->bsd', jax.nn.silu(g) * u, w2)

def rope_tables(positions):
    inv_freq = 1.0 / (ROPE_THETA ** (jnp.arange(0, QK_ROPE_DIM, 2, dtype=jnp.float32) / QK_ROPE_DIM))
    ang = positions.astype(jnp.float32)[..., None] * inv_freq
    return jnp.cos(ang), jnp.sin(ang)

def apply_rope(x, cos, sin):
    xf = x.astype(jnp.float32)
    x1, x2 = jnp.split(xf, 2, axis=-1)
    return jnp.concatenate([x1 * cos - x2 * sin, x2 * cos + x1 * sin], axis=-1).astype(x.dtype)

def causal_mla_attention(q_nope, q_rope, k_nope, k_rope, v):
    b, s, h, _ = q_nope.shape
    nb = s // Q_BLOCK
    scale = (QK_NOPE_DIM + QK_ROPE_DIM) ** -0.5
    key_idx = jnp.arange(s)

    def to_blocks(t):
        return jnp.moveaxis(t.reshape(b, nb, Q_BLOCK, *t.shape[2:]), 1, 0)

    def block(args):
        qn, qr, i = args
        sc = (jnp.einsum('bqhd,bkhd->bhqk', qn, k_nope, preferred_element_type=jnp.float32)
              + jnp.einsum('bqhr,bkr->bhqk', qr, k_rope, preferred_element_type=jnp.float32))
        q_idx = i * Q_BLOCK + jnp.arange(Q_BLOCK)
        mask = key_idx[None, :] <= q_idx[:, None]
        sc = jnp.where(mask, sc * scale, -jnp.inf)
        p = jax.nn.softmax(sc, axis=-1).astype(v.dtype)
        return jnp.einsum('bhqk,bkhd->bqhd', p, v)

    out = lax.map(block, (to_blocks(q_nope), to_blocks(q_rope), jnp.arange(nb)))
    return jnp.moveaxis(out, 0, 1).reshape(b, s, h * V_HEAD_DIM)

def hybrid_mixer(h, cos, sin, w_in, q_a_norm, w_uq, kv_a_norm, w_ukv,
                 q_norm_nope, k_norm_nope, q_norm_rope, k_norm_rope,
                 conv_w, w_branch, w_out):
    b, s, _ = h.shape
    proj = jnp.einsum('bsd,dn->bsn', h, w_in)
    i1 = Q_LORA_RANK
    i2 = i1 + KV_LORA_RANK
    i3 = i2 + QK_ROPE_DIM
    i4 = i3 + 3 * CONV_WIDTH
    c_q, c_kv, k_rope, conv_in, gate_logits = jnp.split(proj, [i1, i2, i3, i4], axis=-1)

    q = jnp.einsum('bsr,rn->bsn', rms_norm(c_q, q_a_norm), w_uq)
    q = q.reshape(b, s, N_HEADS, QK_NOPE_DIM + QK_ROPE_DIM)
    q_nope, q_rope = q[..., :QK_NOPE_DIM], q[..., QK_NOPE_DIM:]
    kv = jnp.einsum('bsr,rn->bsn', rms_norm(c_kv, kv_a_norm), w_ukv)
    kv = kv.reshape(b, s, N_HEADS, QK_NOPE_DIM + V_HEAD_DIM)
    k_nope, v = kv[..., :QK_NOPE_DIM], kv[..., QK_NOPE_DIM:]
    q_nope = rms_norm(q_nope, q_norm_nope)
    k_nope = rms_norm(k_nope, k_norm_nope)
    q_rope = apply_rope(rms_norm(q_rope, q_norm_rope), cos[:, :, None, :], sin[:, :, None, :])
    k_rope = apply_rope(rms_norm(k_rope, k_norm_rope), cos, sin)
    o_attn = causal_mla_attention(q_nope, q_rope, k_nope, k_rope, v)

    xv, gate_b, gate_c = jnp.split(conv_in, 3, axis=-1)
    u = gate_c * xv
    u = lax.conv_general_dilated(u, conv_w[:, None, :], window_strides=(1,),
                                 padding=[(CONV_K - 1, 0)],
                                 dimension_numbers=('NWC', 'WIO', 'NWC'),
                                 feature_group_count=CONV_WIDTH)
    o_conv = gate_b * u

    branches = jnp.stack([o_attn, o_conv], axis=2)
    y_br = jnp.einsum('bsgk,gkd->bsgd', branches, w_branch)
    gates = jax.nn.sigmoid(gate_logits.reshape(b, s, N_BRANCH, D_MODEL))
    merged = jnp.sum(gates * y_br, axis=2)
    return jnp.einsum('bsd,de->bse', merged, w_out)

def first_inputs(seed: int = 0) -> dict:
    key = jax.random.key(seed)
    ks = jax.random.split(key, 20)
    f32 = jnp.float32

    def nrm(k, shape, fan_in):
        return jax.random.normal(k, shape, f32) * (fan_in ** -0.5)

    def gain(k, shape):
        return 1.0 + 0.02 * jax.random.normal(k, shape, f32)

    x = jax.random.normal(ks[0], (BATCH, SEQ, D_MODEL), f32)
    c = jax.random.normal(ks[1], (BATCH, D_MODEL), f32)
    offsets = jax.random.randint(ks[2], (BATCH, 1), 0, 1024, dtype=jnp.int32)
    positions = jnp.arange(SEQ, dtype=jnp.int32)[None, :] + offsets
    return {
        "x": x,
        "c": c,
        "positions": positions,
        "w_ada": nrm(ks[3], (DEPTH, D_MODEL, 3 * N_SUB * D_MODEL), D_MODEL),
        "b_ada": 0.01 * jax.random.normal(ks[4], (DEPTH, 3 * N_SUB * D_MODEL), f32),
        "norm_w": gain(ks[5], (DEPTH, N_SUB, D_MODEL)),
        "ffn_w13": nrm(ks[6], (DEPTH, 2, D_MODEL, 2 * D_FF), D_MODEL),
        "ffn_w2": nrm(ks[7], (DEPTH, 2, D_FF, D_MODEL), D_FF),
        "w_in": nrm(ks[8], (DEPTH, D_MODEL, IN_COLS), D_MODEL),
        "q_a_norm": gain(ks[9], (DEPTH, Q_LORA_RANK)),
        "w_uq": nrm(ks[10], (DEPTH, Q_LORA_RANK, N_HEADS * (QK_NOPE_DIM + QK_ROPE_DIM)), Q_LORA_RANK),
        "kv_a_norm": gain(ks[11], (DEPTH, KV_LORA_RANK)),
        "w_ukv": nrm(ks[12], (DEPTH, KV_LORA_RANK, N_HEADS * (QK_NOPE_DIM + V_HEAD_DIM)), KV_LORA_RANK),
        "q_norm_nope": gain(ks[13], (DEPTH, QK_NOPE_DIM)),
        "k_norm_nope": gain(ks[14], (DEPTH, QK_NOPE_DIM)),
        "q_norm_rope": gain(ks[15], (DEPTH, QK_ROPE_DIM)),
        "k_norm_rope": gain(ks[16], (DEPTH, QK_ROPE_DIM)),
        "conv_w": nrm(ks[17], (DEPTH, CONV_K, CONV_WIDTH), CONV_K),
        "w_branch": nrm(ks[18], (DEPTH, N_BRANCH, BRANCH_WIDTH, D_MODEL), BRANCH_WIDTH),
        "w_out": nrm(ks[19], (DEPTH, D_MODEL, D_MODEL), D_MODEL),
    }

def first_block(x, c, positions, w_ada, b_ada, norm_w, ffn_w13, ffn_w2, w_in,
              q_a_norm, w_uq, kv_a_norm, w_ukv, q_norm_nope, k_norm_nope,
              q_norm_rope, k_norm_rope, conv_w, w_branch, w_out):
    b = x.shape[0]
    cos, sin = rope_tables(positions)
    c_act = jax.nn.silu(c)
    for l in range(DEPTH):
        mod = (jnp.einsum('bd,dn->bn', c_act, w_ada[l]) + b_ada[l]).reshape(b, N_SUB, 3, D_MODEL)
        h = modulate(x, norm_w[l, 0], mod[:, 0, 0], mod[:, 0, 1])
        x = x + 0.5 * mod[:, 0, 2][:, None, :] * swiglu(h, ffn_w13[l, 0], ffn_w2[l, 0])
        h = modulate(x, norm_w[l, 1], mod[:, 1, 0], mod[:, 1, 1])
        y = hybrid_mixer(h, cos, sin, w_in[l], q_a_norm[l], w_uq[l], kv_a_norm[l], w_ukv[l],
                         q_norm_nope[l], k_norm_nope[l], q_norm_rope[l], k_norm_rope[l],
                         conv_w[l], w_branch[l], w_out[l])
        x = x + mod[:, 1, 2][:, None, :] * y
        h = modulate(x, norm_w[l, 2], mod[:, 2, 0], mod[:, 2, 1])
        x = x + 0.5 * mod[:, 2, 2][:, None, :] * swiglu(h, ffn_w13[l, 1], ffn_w2[l, 1])
    return x


DEPTH_2 = 2

GRID_W = 64
CTX_LEN = 256
EXPAND = 2
D_INNER = EXPAND * D_MODEL
HG_HEAD_DIM = 128
HG_HEADS = D_INNER // HG_HEAD_DIM
HG_STREAMS = 5
FT_GROUPS = 8
FT_GROUP_DIM = D_INNER // FT_GROUPS
CHUNK = 64
N_MIXERS = 2
N_HGRN = (DEPTH_2 + 1) // 2
N_FOURIER = DEPTH_2 // 2


def rms_norm_2(x, g):
    xf = x.astype(jnp.float32)
    var = jnp.mean(xf * xf, axis=-1, keepdims=True)
    return (xf * lax.rsqrt(var + EPS)).astype(x.dtype) * g

def adaln(cvec, w, b):
    m = jax.nn.silu(cvec) @ w + b
    return jnp.split(m, 3, axis=-1)

def chunk_scan(q, k, v, g, s0):
    B, H, N, Dk = q.shape
    Dv = v.shape[-1]
    nc = N // CHUNK

    def to_chunks(a):
        a = a.astype(jnp.float32).reshape(B, H, nc, CHUNK, a.shape[-1])
        return jnp.moveaxis(a, 2, 0)

    causal = jnp.tril(jnp.ones((CHUNK, CHUNK), dtype=bool))[:, :, None]

    def step(S, inp):
        qc, kc, vc, gc = inp
        b = jnp.cumsum(gc, axis=-2)
        diff = b[..., :, None, :] - b[..., None, :, :]
        decay = jnp.exp(jnp.where(causal, diff, -jnp.inf))
        scores = jnp.einsum('bhtc,bhtsc,bhsc->bhts', qc, decay, kc)
        o = (jnp.einsum('bhts,bhsv->bhtv', scores, vc)
             + jnp.einsum('bhtc,bhcv->bhtv', qc * jnp.exp(b), S))
        b_last = b[..., -1:, :]
        S_new = (jnp.exp(b_last)[..., 0, :, None] * S
                 + jnp.einsum('bhsc,bhsv->bhcv', kc * jnp.exp(b_last - b), vc))
        return S_new, o

    S_fin, o = lax.scan(step, s0, (to_chunks(q), to_chunks(k), to_chunks(v), to_chunks(g)))
    o = jnp.moveaxis(o, 0, 2).reshape(B, H, N, Dv)
    return o, S_fin

def hgrn_lower_bound(logits, j):
    p = jax.nn.softmax(logits.astype(jnp.float32), axis=0)
    return jnp.cumsum(p, axis=0)[j]

def hgrn_project(h, w_in, lb):
    B, N, _ = h.shape
    p = (h @ w_in).reshape(B, N, HG_STREAMS, HG_HEADS, HG_HEAD_DIM)
    p = jnp.transpose(p, (2, 0, 3, 1, 4))
    q = jax.nn.silu(p[0])
    lbh = lb.reshape(2, 1, HG_HEADS, 1, HG_HEAD_DIM)
    f = lbh + (1.0 - lbh) * jax.nn.sigmoid(p[1:3].astype(jnp.float32))
    return q, 1.0 - f, jnp.log(f), p[3], p[4]

def hgrn_readout(o, z, norm_g, w_out):
    y = rms_norm_2(o, norm_g).astype(z.dtype) * jax.nn.silu(z)
    B, H, N, d = y.shape
    return jnp.transpose(y, (0, 2, 1, 3)).reshape(B, N, H * d) @ w_out

def hgrn_mixer(h_ctx, h_lat, w_in, lb, norm_g, w_out, ctx_out):
    qc, kc, gc, vc, zc = hgrn_project(h_ctx, w_in, lb)
    ql, kl, gl, vl, zl = hgrn_project(h_lat, w_in, lb)
    B = h_lat.shape[0]
    s0 = jnp.zeros((B, HG_HEADS, HG_HEAD_DIM, HG_HEAD_DIM), jnp.float32)
    flip = lambda a: jnp.flip(a, axis=2)
    o_cf, s_cf = chunk_scan(qc, kc[0], vc, gc[0], s0)
    o_cb, s_cb = chunk_scan(flip(qc), flip(kc[1]), flip(vc), flip(gc[1]), s0)
    o_lf, _ = chunk_scan(ql, kl[0], vl, gl[0], s_cf)
    o_lb, _ = chunk_scan(flip(ql), flip(kl[1]), flip(vl), flip(gl[1]), s_cb)
    y_lat = hgrn_readout(o_lf + flip(o_lb), zl, norm_g, w_out)
    y_ctx = hgrn_readout(o_cf + flip(o_cb), zc, norm_g, w_out) if ctx_out else None
    return y_lat, y_ctx

def fourier_mixer(h, w_in, w_out):
    B, N, _ = h.shape
    u, z = jnp.split(h @ w_in, 2, axis=-1)
    ug = u.astype(jnp.float32).reshape(B, N, FT_GROUPS, FT_GROUP_DIM)
    y = jnp.fft.fft2(ug, axes=(1, 3), norm='ortho').real.reshape(B, N, D_INNER)
    return (y.astype(h.dtype) * jax.nn.silu(z)) @ w_out

def second_inputs(seed: int = 0) -> dict:
    key = jax.random.key(seed)
    ks = jax.random.split(key, 14)
    D, E = D_MODEL, D_INNER
    nrm = jax.random.normal
    return {
        'x': nrm(ks[0], (BATCH, SEQ, D), jnp.float32),
        'c': nrm(ks[1], (BATCH, D), jnp.float32),
        'ctx': nrm(ks[2], (BATCH, CTX_LEN, D), jnp.float32),
        'c_ctx': nrm(ks[3], (D,), jnp.float32),
        'ada_w': nrm(ks[4], (DEPTH_2, D, 3 * D), jnp.float32) * (0.5 * D ** -0.5),
        'ada_b': nrm(ks[5], (DEPTH_2, 3 * D), jnp.float32) * 0.01,
        'norm_g': 1.0 + 0.05 * nrm(ks[6], (DEPTH_2, D), jnp.float32),
        'hg_w_in': nrm(ks[7], (N_HGRN, D, HG_STREAMS * E), jnp.float32) * D ** -0.5,
        'hg_lb_logits': 0.5 * nrm(ks[8], (N_HGRN + 1, 2, E), jnp.float32),
        'hg_norm_g': 1.0 + 0.05 * nrm(ks[9], (N_HGRN, HG_HEAD_DIM), jnp.float32),
        'hg_w_out': nrm(ks[10], (N_HGRN, E, D), jnp.float32) * E ** -0.5,
        'ft_w_in': nrm(ks[11], (N_FOURIER, D, 2 * E), jnp.float32) * D ** -0.5,
        'ft_w_out': nrm(ks[12], (N_FOURIER, E, D), jnp.float32) * E ** -0.5,
        'final_g': 1.0 + 0.05 * nrm(ks[13], (D,), jnp.float32),
    }

def second_block(x, c, ctx, c_ctx, ada_w, ada_b, norm_g, hg_w_in, hg_lb_logits, hg_norm_g,
              hg_w_out, ft_w_in, ft_w_out, final_g):
    x_lat, x_ctx = x, ctx
    for i in range(DEPTH_2):
        ctx_out = i < DEPTH_2 - 1
        j = i // N_MIXERS
        sh_l, sc_l, gt_l = adaln(c, ada_w[i], ada_b[i])
        h_lat = rms_norm_2(x_lat, norm_g[i]) * (1.0 + sc_l[:, None]) + sh_l[:, None]
        if i % N_MIXERS == 0:
            sh_c, sc_c, gt_c = adaln(c_ctx, ada_w[i], ada_b[i])
            h_ctx = rms_norm_2(x_ctx, norm_g[i]) * (1.0 + sc_c) + sh_c
            lb = hgrn_lower_bound(hg_lb_logits, j)
            y_lat, y_ctx = hgrn_mixer(h_ctx, h_lat, hg_w_in[j], lb, hg_norm_g[j], hg_w_out[j], ctx_out)
        else:
            y_lat = fourier_mixer(h_lat, ft_w_in[j], ft_w_out[j])
            if ctx_out:
                sh_c, sc_c, gt_c = adaln(c_ctx, ada_w[i], ada_b[i])
                h_ctx = rms_norm_2(x_ctx, norm_g[i]) * (1.0 + sc_c) + sh_c
                y_ctx = fourier_mixer(h_ctx, ft_w_in[j], ft_w_out[j])
        x_lat = x_lat + gt_l[:, None] * y_lat
        if ctx_out:
            x_ctx = x_ctx + gt_c * y_ctx
    return rms_norm_2(x_lat, final_g)


def setup_inputs(seed=0):
    out = dict(first_inputs(seed))
    for name, value in second_inputs(seed + 1).items():
        if name != "x":
            out[name + "_2"] = value
    return out


def reference(
    x, c, positions, w_ada, b_ada, norm_w, ffn_w13, ffn_w2, w_in, q_a_norm, w_uq, kv_a_norm,
    w_ukv, q_norm_nope, k_norm_nope, q_norm_rope, k_norm_rope, conv_w, w_branch, w_out, c_2,
    ctx_2, c_ctx_2, ada_w_2, ada_b_2, norm_g_2, hg_w_in_2, hg_lb_logits_2, hg_norm_g_2,
    hg_w_out_2, ft_w_in_2, ft_w_out_2, final_g_2,
):
    x = first_block(
        x, c, positions, w_ada, b_ada, norm_w, ffn_w13, ffn_w2, w_in, q_a_norm, w_uq, kv_a_norm,
        w_ukv, q_norm_nope, k_norm_nope, q_norm_rope, k_norm_rope, conv_w, w_branch, w_out,
    )
    return second_block(
        x, c_2, ctx_2, c_ctx_2, ada_w_2, ada_b_2, norm_g_2, hg_w_in_2, hg_lb_logits_2,
        hg_norm_g_2, hg_w_out_2, ft_w_in_2, ft_w_out_2, final_g_2,
    )


_drawn_inputs = setup_inputs


def setup_inputs(seed=0):
    import zlib

    import numpy as np

    out = dict(_drawn_inputs(seed))
    spreads = {}
    factors = {'b_ada': 2.951,
     'q_a_norm': 8.0,
     'kv_a_norm': 8.0,
     'q_norm_nope': 8.0,
     'k_norm_nope': 8.0,
     'q_norm_rope': 8.0,
     'k_norm_rope': 8.0,
     'ctx_2': 8.0,
     'c_ctx_2': 8.0,
     'ada_b_2': 7.52,
     'norm_g_2': 4.502,
     'hg_lb_logits_2': 8.0,
     'hg_norm_g_2': 8.0}
    for name, (base, spread) in spreads.items():
        noise = np.random.default_rng([zlib.crc32(name.encode()), seed]).standard_normal(out[name].shape)
        drawn = base * np.exp(spread * noise) if base else spread * noise
        out[name] = __import__('jax').numpy.asarray(drawn.astype(out[name].dtype))
    for name, factor in factors.items():
        out[name] = (out[name] * factor).astype(out[name].dtype)
    return out
```

```python
from contextlib import ExitStack

import numpy as np

import concourse.bass as bass
from concourse import mybir

ALU = mybir.AluOpType
ACT = mybir.ActivationFunctionType
AX = mybir.AxisListType
F32 = mybir.dt.float32
F32R = mybir.dt.float32r
I32 = mybir.dt.int32
U8 = mybir.dt.uint8

P = 128
T, TC = 512, 256
D = 1024
KD = D // P
FF = 2816
KF = FF // P
W2S = 3
HEADS, DN, DR, DV = 8, 64, 32, 64
QR, KVR = 256, 128
CW = 512
HG = 16
FG = 8
EPS = 1e-6
EXP_LN = "natural_log_exp_and_others"
ATT_SCALE = float((DN + DR) ** -0.5)
NEG = -3.0e38

RING = 3
LEAD = 2
N_FFN = 2 * KF + KD * W2S
N_IN = 4
N_CONV = 12
N_UP = 3
N_GB = 3 * KD
N_OUT = KD
S_FFN1 = 0
S_MIX = S_FFN1 + N_FFN
S_FFN2 = S_MIX + N_IN + N_CONV + N_UP + N_GB + N_OUT
S_HG = S_FFN2 + N_FFN
S_FT = S_HG + 6 * HG
S_END = S_FT + 6 * FG
N_SLOTS = S_END
ADA_RING = 4

N_VEC = 17

COLS = {}
_at = 0
for _name, _n in (("bias", 8 * N_VEC), ("c", 24), ("norm_w", 24), ("norm_g2", 16), ("final_g", 8), ("qa", 2),
                  ("kva", 1), ("qe", 1), ("qo", 1), ("kn", 1), ("kr", 1), ("conv", 12), ("hg_norm", 1),
                  ("lb", 64), ("inv_freq", 1)):
    COLS[_name] = (_at, _n)
    _at += _n
N_COLS = _at

CONST = {n: i for i, n in enumerate(("ident", "ones", "bd_even", "bd_odd", "bd_k", "bd_rope", "rot", "causal"))}
LEVELS = (1, 2, 4, 8, 16, 32, 64)


def build(nc, ws, ada, colsd, constd, maskd, dftcd, dftsd, xd, ctxd, posd, out):
    with ExitStack() as ctx:
        def sem(name):
            return ctx.enter_context(nc.semaphore(name))

        def sb(name, shape, dt=F32, where=ctx):
            return where.enter_context(nc.sbuf_tensor(name, shape, dt))

        raw = sb("raw", [P, RING, D])
        wh = sb("wh", [P, RING, D], F32R)
        wl = sb("wl", [P, RING, D], F32R)
        xT = sb("xT", [P, KD, T])
        hH = sb("hH", [P, KD, T], F32R)
        hL = sb("hL", [P, KD, T], F32R)
        sq = sb("sq", [P, T])
        acc = sb("acc", [P, T])
        rs = sb("rs", [P, T])
        cols = sb("cols", [P, N_COLS])
        cst = sb("cst", [P, len(CONST), P])
        mod = cols[:, COLS["bias"][0]:COLS["bias"][0] + 8 * N_VEC]
        cact = sb("cact", [P, 24])
        coef = sb("coef", [P, 8])
        gain = sb("gain", [P, 8])
        red = sb("red", [P, 8])
        epsc = sb("epsc", [P, 1])
        nt = sb("nt", [P, 2, T])
        sil, s32 = nt[:, 0, :], nt[:, 1, :]

        with ExitStack() as ph:
            sH = sb("sH", [P, KF, T], F32R, ph)
            sL = sb("sL", [P, KF, T], F32R, ph)
            araw = sb("araw", [P, ADA_RING, D], F32, ph)
            aacc = sb("aacc", [P, D], F32, ph)
        with ExitStack() as ph:
            xin = sb("xin", [P, 4, D], F32, ph)
            praw = sb("praw", [P, 8, D], F32, ph)
            pacc = sb("pacc", [P, 2, D], F32, ph)
        ps = ctx.enter_context(nc.psum_tensor("ps", [P, 8, T], F32))

        def col(name, i=0, n=1):
            return cols[:, COLS[name][0] + i:COLS[name][0] + i + n]

        def const(name):
            return cst[:, CONST[name], :]

        loaded = [sem(f"loaded{i}") for i in range(RING)]
        hi_ready = sem("hi_ready")
        lo_ready = sem("lo_ready")
        slot_done = sem("slot_done")
        s_small = sem("s_small")
        s_x = sem("s_x")
        s_praw = [sem(f"s_praw{i}") for i in range(8)]
        s_cact = sem("s_cact")
        s_pacc = sem("s_pacc")
        xt_t = sem("xt_t")
        xt_c = sem("xt_c")
        setup = sem("setup")
        ada_ld = [sem(f"ada_ld{i}") for i in range(ADA_RING)]
        ada_step = sem("ada_step")
        paced = sem("paced")
        paced_dve = sem("paced_dve")
        ada_t = sem("ada_t")
        ada_r = sem("ada_r")
        sq_done = sem("sq_done")
        acc_step = sem("acc_step")
        ms_done = sem("ms_done")
        rs_step = sem("rs_step")
        gain_done = sem("gain_done")
        nt_done = sem("nt_done")
        nh_done = sem("nh_done")
        nl_done = sem("nl_done")
        sil_done = sem("sil_done")
        ffn_mul = sem("ffn_mul")
        ffn_h = sem("ffn_h")
        ffn_l = sem("ffn_l")
        resid = sem("resid")
        coef_done = sem("coef_done")
        fin_t = sem("fin_t")
        fin_c = sem("fin_c")
        s_out = sem("s_out")

        def at(s, g=0, per=0):
            return s + g * per

        def split_hi(act, s, g=0, per=0):
            j, n = s % RING, at(s, g, per)
            act.wait_ge(loaded[j], at(16 * (s // RING + 1), g, 16 * per // RING))
            act.wait_ge(slot_done, n + 1)
            act.activation(wh[:, j, :], raw[:, j, :], ACT.Copy).then_inc(hi_ready, 1)

        def split_lo(dve, s, g=0, per=0):
            j, n = s % RING, at(s, g, per)
            dve.wait_ge(hi_ready, n + 1)
            dve.tensor_tensor(wl[:, j, :], raw[:, j, :], wh[:, j, :].bitcast(F32), ALU.subtract).then_inc(lo_ready, 1)

        def products(pe, o, a_hi, a_lo, b_hi, b_lo, start, stop, **kw):
            pe.matmul(o, a_hi, b_hi, start=start, stop=False, **kw)
            pe.matmul(o, a_hi, b_lo, start=False, stop=False, **kw)
            return pe.matmul(o, a_lo, b_hi, start=False, stop=stop, **kw)

        def slot_ready(pe, s, g=0, per=0):
            pe.wait_ge(lo_ready, at(s, g, per) + RING + 1)

        def wait_slot(eng, s, g=0, per=0):
            eng.wait_ge(slot_done, at(s, g, per) + RING + 1)

        def gemm(pe, o, s, g, per, xh, xl, first=None):
            j = s % RING
            slot_ready(pe, s, g, per)
            for k in range(KD):
                if first is not None:
                    pe.wait_ge(nl_done, first + k + 1)
                w = slice(k * P, (k + 1) * P)
                last = products(pe, o, wh[:, j, w], wl[:, j, w], xh[:, k, :], xl[:, k, :], k == 0, k == KD - 1)
            return last

        def norm_pe(pe, m, bank, n=T):
            pe.wait_ge(acc_step, 9 * m + 9)
            pe.matmul(ps[:, bank, 0:n], const("ones"), acc[:, 0:n], start=True, stop=True).then_inc(ms_done, 1)

        def norm_act(act, m, bank, shift, n=T, dst=hH):
            act.preload_act_table_set(EXP_LN)
            act.wait_ge(ms_done, m + 1)
            act.activation(rs[:, 0:n], ps[:, bank, 0:n], ACT.Ln, bias=epsc[:, :], scale=1.0 / D).then_inc(rs_step, 1)
            act.wait_ge(rs_step, 2 * m + 1)
            act.activation(rs[:, 0:n], rs[:, 0:n], ACT.Exp, scale=-0.5).then_inc(rs_step, 1)
            for k in range(KD):
                act.wait_ge(nt_done, 8 * m + k + 1)
                act.activation(dst[:, k, 0:n], nt[:, k % 2, 0:n], ACT.Identity, bias=shift[:, k:k + 1]).then_inc(nh_done, 1)

        def norm_gain(dve, m, w, scale):
            if m:
                dve.wait_ge(nt_done, 8 * m)
            dve.scalar_tensor_tensor(gain[:, :], scale, 1.0, w, ALU.add, ALU.mult).then_inc(gain_done, 1)

        def norm_dve(dve, m, shift, n=T, dh=hH, dl=hL, src=xT):
            dve.wait_ge(rs_step, 2 * m + 2)
            dve.wait_ge(gain_done, m + 1)

            def scaled(k):
                if 8 * m + k >= 2:
                    dve.wait_ge(nl_done, 8 * m + k - 1)
                dve.scalar_tensor_tensor(nt[:, k % 2, 0:n], src[:, k, 0:n], gain[:, k:k + 1], rs[:, 0:n],
                                         ALU.mult, ALU.mult).then_inc(nt_done, 1)

            scaled(0)
            for k in range(KD):
                if k + 1 < KD:
                    scaled(k + 1)
                dve.wait_ge(nh_done, 8 * m + k + 1)
                dve.scalar_tensor_tensor(dl[:, k, 0:n], nt[:, k % 2, 0:n], shift[:, k:k + 1],
                                         dh[:, k, 0:n].bitcast(F32), ALU.add, ALU.subtract).then_inc(nl_done, 1)

        def acc_clear(dve, m):
            if m:
                dve.wait_ge(ms_done, m)
            dve.memset(acc[:, :], 0.0).then_inc(acc_step, 1)

        def acc_add(dve, m, k, n=T):
            dve.wait_ge(sq_done, 8 * m + k + 1)
            dve.wait_ge(acc_step, 9 * m + k + 1)
            dve.tensor_tensor(acc[:, 0:n], acc[:, 0:n], sq[:, 0:n], ALU.add).then_inc(acc_step, 1)

        def square(act, m, k, src, n=T):
            act.wait_ge(acc_step, 9 * m + k + 1)
            act.activation(sq[:, 0:n], src, ACT.Square).then_inc(sq_done, 1)

        def resid_dve(dve, r, bank, o, m):
            dve.wait_ge(coef_done, 1)
            xo = xT[:, bass.ds(o, 1), :].rearrange("p a t -> p (a t)") if not isinstance(o, int) else xT[:, o, :]
            co = coef[:, bass.ds(o, 1)] if not isinstance(o, int) else coef[:, o:o + 1]
            dve.scalar_tensor_tensor(xo, ps[:, bank, :], co, xo, ALU.mult, ALU.add).then_inc(resid, 1)

        def pick(t, o):
            return t[:, o, :] if isinstance(o, int) else t[:, bass.ds(o, 1), :].rearrange("p a t -> p (a t)")

        def collect_pe(pe, job):
            pe.wait_ge(ada_step, 8 * job + 8 + ADA_RING)
            pe.wait_ge(ada_r, 3 * job + 6)
            for j in range(KD):
                last = pe.transpose(ps[:, 6 + j // 4, (j % 4) * P:(j % 4 + 1) * P], aacc[:, j * P:(j + 1) * P], const("ident"))
            last.then_inc(ada_t, 1)

        def collect_dve(dve, c, v):
            dve.wait_ge(ada_t, c + 1)
            if not (isinstance(c, int) and c == 0):
                dve.wait_ge(ada_r, 3 * c)
            for b in range(2):
                dve.tensor_reduce(red[:, 4 * b:4 * b + 4], ps[:, 6 + b, :].rearrange("p (j k) -> p j k", k=P),
                                  AX.X, ALU.add).then_inc(ada_r, 1)
            dve.wait_ge(ada_r, 3 * c + 2)
            if isinstance(v, int):
                dst = mod[:, 8 * v:8 * v + 8]
            else:
                dst = mod.rearrange("p (v j) -> p v j", j=8)[:, bass.ds(v, 1), :].rearrange("p v j -> p (v j)")
            dve.tensor_tensor(dst, red[:, :], dst, ALU.add).then_inc(ada_r, 1)

        JOBS = (7, 8)

        def ffn_pair_pe(pe, i, s0, p, g, first):
            q = at(p, g, 3)
            pe.wait_ge(ffn_mul, KF * i + q + 1)
            for u in range(2):
                last = gemm(pe, ps[:, 2 * p + u, :], s0 + 2 * p + u, g, 6, hH, hL, first if (p == 0 and u == 0) else None)
                last.then_inc(slot_done, 1)

        def ffn_pe(pe, i, s0, m):
            with pe.Fori(0, 7) as g:
                for p in range(3):
                    ffn_pair_pe(pe, i, s0, p, g, 8 * m)
                collect_pe(pe, at(JOBS[0] * i, g, 1))
            pe.wait_ge(ffn_mul, KF * i + 22)
            for u in range(2):
                gemm(pe, ps[:, u, :], s0 + 42 + u, 0, 0, hH, hL).then_inc(slot_done, 1)
            with pe.Fori(0, 4) as g:
                for t in range(2):
                    pe.wait_ge(resid, at(RB[i] + t + 1, g, 2))
                    for w in range(W2S):
                        s = s0 + 44 + 3 * t + w
                        slot_ready(pe, s, g, 6)
                        hi = min(KF, 8 * w + 8)
                        pe.wait_ge(ffn_l, KF * i + hi + 1)
                        for k in range(8 * w, hi):
                            c = slice((k - 8 * w) * P, (k - 8 * w + 1) * P)
                            last = products(pe, ps[:, 2 + t, :], wh[:, s % RING, c], wl[:, s % RING, c],
                                            sH[:, k, :], sL[:, k, :], k == 0, k == KF - 1)
                        last.then_inc(slot_done, 1)
            if i == 1:
                collect_pe(pe, 14)

        def ffn_act(act, i, s0, m):
            def pair(p, g, s):
                q = at(p, g, 3)
                split_hi(act, s + LEAD, g, 6)
                wait_slot(act, s, g, 6)
                act.wait_ge(ffn_mul, KF * i + q + 3)
                act.activation(sil, ps[:, 2 * (p % 3), :], ACT.Silu).then_inc(sil_done, 1)
                split_hi(act, s + 1 + LEAD, g, 6)
                act.wait_ge(ffn_mul, KF * i + q + 4)
                act.activation(pick(sH, q), s32, ACT.Copy).then_inc(ffn_h, 1)
            with act.Fori(0, 7) as g:
                for p in range(3):
                    pair(p, g, s0 + 2 * p)
            pair_last = KF - 1
            split_hi(act, s0 + 42 + LEAD)
            wait_slot(act, s0 + 42)
            act.wait_ge(ffn_mul, KF * i + pair_last + 3)
            act.activation(sil, ps[:, 0, :], ACT.Silu).then_inc(sil_done, 1)
            split_hi(act, s0 + 43 + LEAD)
            act.wait_ge(ffn_mul, KF * i + pair_last + 4)
            act.activation(sH[:, pair_last, :], s32, ACT.Copy).then_inc(ffn_h, 1)
            with act.Fori(0, 4) as g:
                for t in range(2):
                    for w in range(W2S):
                        split_hi(act, s0 + 44 + 3 * t + w + LEAD, g, 6)
                    o = at(t, g, 2)
                    act.wait_ge(resid, RB[i] + o + 3)
                    act.wait_ge(acc_step, 9 * (m + 1) + o + 1)
                    act.activation(sq[:, :], pick(xT, o), ACT.Square).then_inc(sq_done, 1)

        def ffn_dve(dve, i, s0, m):
            def pair(p, g, s, q, between=None):
                split_lo(dve, s + LEAD, g, 6)
                split_lo(dve, s + 1 + LEAD, g, 6)
                if between:
                    between()
                dve.wait_ge(sil_done, KF * i + q + 1)
                wait_slot(dve, s + 1, g, 6)
                dve.wait_ge(ffn_l, KF * i + q + 1)
                dve.tensor_tensor(s32, sil, ps[:, 2 * p + 1, :], ALU.mult).then_inc(ffn_mul, 1)
                dve.wait_ge(ffn_h, KF * i + q + 1)
                dve.tensor_tensor(pick(sL, q), s32, pick(sH, q).bitcast(F32), ALU.subtract).then_inc(ffn_l, 1)

            def three(g, c):
                job = at(JOBS[0] * i, g, 1)
                for p in range(3):
                    pair(p, g, s0 + 2 * p, at(p, g, 3), lambda: ada_sum(dve, job, c, 3 * p, min(3 * p + 3, KD)))
                collect_dve(dve, at(2, job, 1), at(2, job, 1))

            with dve.Fori(0, 7 - i) as g:
                three(g, 8 * i)
            if i == 1:
                three(6, 16)
            pair(0, 0, s0 + 42, KF - 1)
            dve.wait_ge(ada_r, (27, 48)[i])
            if i:
                dve.wait_ge(resid, RB[i] + 2)
            dve.tensor_scalar(coef[:, :], mod[:, 8 * (6 * i + 2):8 * (6 * i + 3)], 0.5, None, ALU.mult).then_inc(coef_done, 1)
            acc_clear(dve, m + 1)
            dve.wait_ge(coef_done, CB[i] + 1)
            if i == 1:
                ada_sum(dve, 14, 16, 0, KD)
            with dve.Fori(0, 4) as g:
                for t in range(2):
                    for w in range(W2S):
                        split_lo(dve, s0 + 44 + 3 * t + w + LEAD, g, 6)
                    o = at(t, g, 2)
                    wait_slot(dve, s0 + 44 + 3 * t + 2, g, 6)
                    dve.scalar_tensor_tensor(pick(xT, o), ps[:, 2 + t, :], coef[:, bass.ds(o, 1)], pick(xT, o),
                                             ALU.mult, ALU.add).then_inc(resid, 1)
                    dve.wait_ge(sq_done, 8 * (m + 1) + o + 1)
                    dve.wait_ge(acc_step, 9 * (m + 1) + o + 1)
                    dve.tensor_tensor(acc[:, :], acc[:, :], sq[:, :], ALU.add).then_inc(acc_step, 1)
            if i == 1:
                collect_dve(dve, 16, 16)

        def ada_load(pool, job, v, src):
            for k in range(KD):
                w = src[v * 8 + k] if isinstance(v, int) else src.rearrange("(v k) p n -> v k p n", k=8)[bass.ds(v, 1), k].rearrange("v p n -> (v p) n")
                pool.wait_ge(ada_step, 8 * job + k + 1)
                pool.dma_start(araw[:, k % ADA_RING, :], w).then_inc(ada_ld[k % ADA_RING], 16)

        def ada_sum(dve, job, c, lo, hi):
            per = KD // ADA_RING
            for k in range(lo, hi):
                dve.wait_ge(ada_ld[k % ADA_RING], 16 * per * job + 16 * (k // ADA_RING + 1))
                f = cact[:, c + k:c + k + 1]
                if k == 0:
                    dve.wait_ge(ada_t, job + 2)
                    dve.tensor_scalar(aacc[:, :], araw[:, 0, :], f, None, ALU.mult).then_inc(ada_step, 1)
                else:
                    dve.wait_ge(ada_step, 8 * job + k + ADA_RING)
                    dve.scalar_tensor_tensor(aacc[:, :], araw[:, k % ADA_RING, :], f, aacc[:, :],
                                             ALU.mult, ALU.add).then_inc(ada_step, 1)

        RB = (0, 2 * KD)
        CB = (0, 1)

        with ExitStack() as ph:
            vT = sb("vT", [P, 4, T], F32, ph)
            oaH = sb("oaH", [P, 4, T], F32R, ph)
            oaL = sb("oaL", [P, 4, T], F32R, ph)
            ocH = sb("ocH", [P, 4, T], F32R, ph)
            ocL = sb("ocL", [P, 4, T], F32R, ph)
            cosT = sb("cosT", [P, T], F32, ph)
            sinT = sb("sinT", [P, T], F32, ph)
            cu = sb("cu", [P, T + 2], F32, ph)
            cy = sb("cy", [P, T], F32, ph)
            sg = sb("sg", [P, 2, T], F32, ph)
            csq, crs = sg, nt
            with ExitStack() as p2:
                qT = sb("qT", [P, HEADS, T], F32, p2)
                kT = sb("kT", [P, HEADS, T], F32, p2)
                with ExitStack() as p3:
                    c32 = sb("c32", [P, 4, T], F32, p3)
                    cH = sb("cH", [P, 3, T], F32R, p3)
                    cL = sb("cL", [P, 3, T], F32R, p3)
                with ExitStack() as p3:
                    pr = sb("pr", [P, 2, 1280], F32, p3)
                    pt = sb("pt", [P, 2, 1280], F32, p3)
                    st = sb("st", [P, 2, 16], F32, p3)
            with ExitStack() as p2:
                mH = sb("mH", [P, KD, T], F32R, p2)
                mL = sb("mL", [P, KD, T], F32R, p2)

        c_sq = sem("c_sq")
        c_ms = sem("c_ms")
        c_rs = sem("c_rs")
        c_n = sem("c_n")
        c_h = sem("c_h")
        c_l = sem("c_l")
        kr_rot = sem("kr_rot")
        kr_step = sem("kr_step")
        s_pos = sem("s_pos")
        tb_step = sem("tb_step")
        tb_sin = sem("tb_sin")
        up_t = sem("up_t")
        up_sq = sem("up_sq")
        up_ms = sem("up_ms")
        up_rs = sem("up_rs")
        up_n = sem("up_n")
        up_rot = sem("up_rot")
        up_r = sem("up_r")
        up_v = sem("up_v")
        up_vc = sem("up_vc")
        cv_g = sem("cv_g")
        cv_step = sem("cv_step")
        cv_h = sem("cv_h")
        at_s = sem("at_s")
        at_m = sem("at_m")
        at_e = sem("at_e")
        at_p = sem("at_p")
        at_t = sem("at_t")
        at_c = sem("at_c")
        at_o = sem("at_o")
        at_h = sem("at_h")
        at_l = sem("at_l")
        gb_s = sem("gb_s")
        gb_m = sem("gb_m")
        gb_h = sem("gb_h")
        gb_l = sem("gb_l")

        B0 = S_MIX
        B_CONV = [B0 + N_IN] + [B0 + N_IN + 3 + N_UP + 3 * c for c in range(3)]
        B_UP = B0 + N_IN + 3
        B_GB = B0 + N_IN + N_CONV + N_UP
        B_OUT = B_GB + N_GB
        CB_BANKS = ((4, 5, 6), (3, 4, 5), (3, 4, 5), (3, 4, 5))
        POFF = (0, 128, 384, 768)
        TOFF = (0, 512, 896, 1152)
        S_BANK = ((1, 384), (2, 0), (1, 0), (0, 0))
        T_BANK = ((6, 0), (1, 0), (2, 0), (1, 384))

        S_ORDER, S_NEED = (3, 2, 0, 1), (1, 3, 3, 4)
        T_ORDER, T_NEED = (0, 2, 1, 3), (1, 2, 4, 4)

        def rows(h):
            return slice(64, 96) if h % 2 == 0 else slice(0, 32)

        def conv_slot_pe(pe, c, u):
            s = B_CONV[c] + u
            if u == 0 and c >= 1:
                pe.wait_ge(cv_step, 7 * c + 1)
            gemm(pe, ps[:, CB_BANKS[c][u], :], s, 0, 0, hH, hL).then_inc(slot_done, 1)

        def scores_pe(pe, h):
            if h >= 1:
                pe.wait_ge(at_c, 4 * h)
            for i in S_ORDER:
                b, c0 = S_BANK[i]
                pe.matmul(ps[:, b, c0:c0 + (i + 1) * P], qT[:, h, i * P:(i + 1) * P], kT[:, h, 0:(i + 1) * P],
                          start=True, stop=True, skip_group_check=True).then_inc(at_s, 1)

        def values_pe(pe, h):
            pe.wait_ge(at_p, 5 * h + 5)
            for j in T_ORDER:
                b, c0 = T_BANK[j]
                for i in range(j, 4):
                    last = pe.transpose(ps[:, b, c0 + (i - j) * P:c0 + (i - j + 1) * P],
                                        pr[:, h % 2, POFF[i] + j * P:POFF[i] + (j + 1) * P], const("ident"))
                last.then_inc(at_t, 1)
            if h % 2 == 0 and h >= 2:
                pe.wait_ge(at_l, h // 2)
            r = slice(64 * (h % 2), 64 * (h % 2) + 64)
            for n, j in enumerate(T_ORDER):
                pe.wait_ge(at_c, 4 * h + n + 1)
                last = pe.matmul(ps[r, 7, j * P:T], vT[:, j, h * DV:(h + 1) * DV], pt[:, h % 2, TOFF[j]:TOFF[j] + T - j * P],
                                 start=(n == 0), stop=(n == 3), skip_group_check=True)
            last.then_inc(at_o, 1)

        def mix_pe(pe):
            norm_pe(pe, 1, 7)
            for i in range(4):
                gemm(pe, ps[:, i, :], B0 + i, 0, 0, hH, hL, 8 if i == 0 else None).then_inc(slot_done, 1)
            for i in range(4):
                if i % 2 == 0:
                    conv_slot_pe(pe, 0, i // 2)
                pe.wait_ge(c_sq, 2 * i + 2)
                pe.matmul(ps[:, (7, 7, 0, 1)[i], :], const("bd_rope" if i == 3 else "ones"), csq[:, i % 2, :],
                          start=(i != 1), stop=(i != 0)).then_inc(c_ms, 1)
            conv_slot_pe(pe, 0, 2)
            pe.wait_ge(c_n, 4)
            pe.matmul(ps[:, 2, :], const("rot"), c32[:, 3, :], start=True, stop=True).then_inc(kr_rot, 1)

            def tile(t):
                s = B_UP + t // 4
                if t % 4 == 0:
                    slot_ready(pe, s)
                pe.wait_ge(c_l, 3 if t >= 8 else 2)
                if t < 3:
                    pe.wait_ge(kr_step, 3)
                else:
                    pe.wait_ge(up_n, t - 2)
                j, o = s % RING, ps[:, t % 3, :]
                if t < 8:
                    for k in range(2):
                        c = slice((2 * (t % 4) + k) * P, (2 * (t % 4) + k + 1) * P)
                        last = products(pe, o, wh[:, j, c], wl[:, j, c], cH[:, k, :], cL[:, k, :], k == 0, k == 1)
                else:
                    c = slice((t - 8) * P, (t - 7) * P)
                    last = products(pe, o, wh[:, j, c], wl[:, j, c], cH[:, 2, :], cL[:, 2, :], True, True)
                last.then_inc(up_t, 1)

            def mean_square(t):
                pe.wait_ge(up_sq, t + 1)
                if t >= 2:
                    pe.wait_ge(up_rs, 2 * t - 3)
                name = "bd_k" if t >= 8 else ("bd_even", "bd_odd")[t % 2]
                pe.matmul(ps[:, 3 + t % 2, :], const(name), csq[:, t % 2, :], start=True, stop=True).then_inc(up_ms, 1)

            def rotate(t):
                pe.wait_ge(up_n, t + 1)
                if t >= 2:
                    pe.wait_ge(up_r, 3 * (t - 2) + 3)
                pe.matmul(ps[:, 5 + t % 2, :], const("rot"), qT[:, t, :], start=True, stop=True).then_inc(up_rot, 1)

            pe.wait_ge(cv_step, 8)
            for t in range(14):
                if t < 12:
                    tile(t)
                if 1 <= t <= 12:
                    mean_square(t - 1)
                if 2 <= t <= 9:
                    rotate(t - 2)
                if t == 3 or t == 7:
                    pe.drain().then_inc(slot_done, 1)
            j = (B_UP + 2) % RING
            for a in range(4):
                if a < 2:
                    pe.wait_ge(up_r, 24)
                else:
                    pe.wait_ge(up_vc, a - 1)
                c = slice(a * P, (a + 1) * P)
                last = products(pe, ps[:, 5 + a % 2, :], cH[:, 2, c], cL[:, 2, c], wh[:, j, 512:], wl[:, j, 512:], True, True)
                last.then_inc(up_v, 1)
            pe.drain().then_inc(slot_done, 1)
            pe.wait_ge(up_n, 12)
            pe.wait_ge(kr_step, 5)
            pe.wait_ge(up_vc, 4)
            pe.wait_ge(up_rs, 24)
            for h in range(HEADS):
                scores_pe(pe, h)
                conv_slot_pe(pe, 1 + h // 3, h % 3)
                values_pe(pe, h)
            conv_slot_pe(pe, 3, 2)
            pe.wait_ge(at_l, 4)
            pe.wait_ge(cv_step, 29)
            with pe.Fori(0, 4) as g:
                for t in range(2):
                    o, b = at(t, g, 2), 4 * t
                    pe.wait_ge(gb_m, 3 * o + 3)
                    for u in range(2):
                        gemm(pe, ps[:, b + u, :], B_GB + 3 * t + u, g, 6, hH, hL).then_inc(slot_done, 1)
                    s = B_GB + 3 * t + 2
                    slot_ready(pe, s, g, 6)
                    for k in range(KD):
                        c = slice(k * P, (k + 1) * P)
                        xh, xl = (oaH, oaL) if k < 4 else (ocH, ocL)
                        last = products(pe, ps[:, b + 2 + k // 4, :], wh[:, s % RING, c], wl[:, s % RING, c],
                                        xh[:, k % 4, :], xl[:, k % 4, :], k % 4 == 0, k % 4 == 3)
                    last.then_inc(slot_done, 1)
            pe.wait_ge(gb_m, 3 * KD + 6)
            for o in range(KD):
                s = B_OUT + o
                slot_ready(pe, s)
                for k in range(KD):
                    pe.wait_ge(gb_l, k + 2)
                    c = slice(k * P, (k + 1) * P)
                    last = products(pe, ps[:, o, :], wh[:, s % RING, c], wl[:, s % RING, c], mH[:, k, :], mL[:, k, :],
                                    k == 0, k == KD - 1)
                last.then_inc(slot_done, 1)

        def conv_gate_act(act, c):
            wait_slot(act, B_CONV[c] + 2)
            act.wait_ge(cv_step, 7 * c + 1)
            act.activation(cy[:, :], ps[:, CB_BANKS[c][2], :], ACT.Copy).then_inc(cv_g, 1)

        def conv_high_act(act, c):
            act.wait_ge(cv_step, 7 * c + 7)
            act.activation(ocH[:, c, :], cy[:, :], ACT.Copy).then_inc(cv_h, 1)

        def mix_act(act):
            norm_act(act, 1, 7, mod[:, 24:32])
            act.wait_ge(tb_step, 9)
            act.activation(sinT[:, :], cosT[:, :], ACT.Sin).then_inc(tb_sin, 1)
            act.activation(cosT[:, :], cosT[:, :], ACT.Abs).then_inc(tb_sin, 1)
            act.wait_ge(tb_step, 10)
            act.activation(cosT[:, :], cosT[:, :], ACT.Sin).then_inc(tb_sin, 1)
            for i in range(4):
                split_hi(act, B0 + i + LEAD)
                wait_slot(act, B0 + i)
                act.activation(c32[:, i, :], ps[:, i, :], ACT.Copy).then_inc(c_sq, 1)
                if i >= 2:
                    act.wait_ge(c_ms, i - 1)
                act.activation(csq[:, i % 2, :], ps[:, i, :], ACT.Square).then_inc(c_sq, 1)
            split_hi(act, B_CONV[0] + LEAD)

            def inv_rms(n, bank, scale, done, ready, at_n):
                act.wait_ge(ready, at_n)
                act.preload_act_table_set(EXP_LN)
                act.activation(crs[:, n % 2, :], ps[:, bank, :], ACT.Ln, bias=epsc[:, :], scale=scale).then_inc(done, 1)
                act.wait_ge(done, 2 * n + 1)
                act.activation(crs[:, n % 2, :], crs[:, n % 2, :], ACT.Exp, scale=-0.5).then_inc(done, 1)

            inv_rms(0, 7, 1.0 / QR, c_rs, c_ms, 2)
            inv_rms(1, 0, 1.0 / KVR, c_rs, c_ms, 3)
            act.wait_ge(c_n, 2)
            inv_rms(2, 1, 1.0, c_rs, c_ms, 4)
            for i in range(3):
                act.wait_ge(c_n, i + 1)
                act.activation(cH[:, i, :], c32[:, i, :], ACT.Copy).then_inc(c_h, 1)
            split_hi(act, B_CONV[0] + 1 + LEAD)
            split_hi(act, B_CONV[0] + 2 + LEAD)
            conv_gate_act(act, 0)
            conv_high_act(act, 0)
            def up_square(t):
                act.wait_ge(up_t, t + 1)
                if t >= 2:
                    act.wait_ge(up_ms, t - 1)
                else:
                    act.wait_ge(c_ms, 4)
                act.activation(csq[:, t % 2, :], ps[:, t % 3, :], ACT.Square).then_inc(up_sq, 1)

            for t in range(13):
                if t < 12:
                    up_square(t)
                if t >= 1:
                    act.wait_ge(up_n, t - 2) if t > 2 else act.wait_ge(c_n, 4)
                    inv_rms(t - 1, 3 + (t - 1) % 2, 1.0, up_rs, up_ms, t)
                if t == 4:
                    split_hi(act, B_UP + LEAD)
                if t == 8:
                    split_hi(act, B_UP + 1 + LEAD)
            for a in range(4):
                act.wait_ge(up_v, a + 1)
                act.activation(vT[:, a, :], ps[:, 5 + a % 2, :], ACT.Copy).then_inc(up_vc, 1)
            split_hi(act, B_UP + 2 + LEAD)
            for h in range(HEADS):
                for i in S_ORDER:
                    act.wait_ge(at_m, 9 * h + 9)
                    if h >= 2:
                        act.wait_ge(at_t, 4 * (h - 1))
                    b, c0 = S_BANK[i]
                    act.activation(pr[:, h % 2, POFF[i]:POFF[i] + (i + 1) * P], ps[:, b, c0:c0 + (i + 1) * P], ACT.Exp,
                                   bias=st[:, h % 2, 4 + i:5 + i], scale=ATT_SCALE,
                                   accum_out=st[:, h % 2, 8 + i:9 + i]).then_inc(at_e, 1)
                split_hi(act, B_CONV[1] + h + LEAD)
                if h % 3 == 2:
                    conv_gate_act(act, 1 + h // 3)
                for n, j in enumerate(T_ORDER):
                    act.wait_ge(at_t, 4 * h + T_NEED[n])
                    if h >= 2:
                        act.wait_ge(at_o, h - 1)
                    b, c0 = T_BANK[j]
                    act.activation(pt[:, h % 2, TOFF[j]:TOFF[j] + T - j * P], ps[:, b, c0:c0 + T - j * P], ACT.Copy).then_inc(at_c, 1)
                if h % 2 == 1:
                    act.wait_ge(at_o, h + 1)
                    act.activation(oaH[:, h // 2, :], ps[:, 7, :], ACT.Copy).then_inc(at_h, 1)
                if h % 3 == 2:
                    conv_high_act(act, 1 + h // 3)
            split_hi(act, B_CONV[1] + 8 + LEAD)
            conv_gate_act(act, 3)
            conv_high_act(act, 3)
            with act.Fori(0, 4) as g:
                for t in range(2):
                    o = at(t, g, 2)
                    for u in range(2):
                        s = B_GB + 3 * t + u
                        split_hi(act, s + LEAD, g, 6)
                        wait_slot(act, s, g, 6)
                        act.wait_ge(gb_m, 3 * o + 6)
                        act.activation(sg[:, u, :], ps[:, 4 * t + u, :], ACT.Sigmoid).then_inc(gb_s, 1)
                    split_hi(act, B_GB + 3 * t + 2 + LEAD, g, 6)
                    act.wait_ge(gb_m, 3 * o + 9)
                    act.activation(pick(mH, o), cy[:, :], ACT.Copy).then_inc(gb_h, 1)
            for o in range(KD):
                split_hi(act, B_OUT + o + LEAD)
                act.wait_ge(resid, 8 + o + 3)
                square(act, 2, o, xT[:, o, :])

        def conv_dve(dve, c):
            b = CB_BANKS[c]
            base = 7 * c + 1
            dve.wait_ge(cv_g, c + 1)
            dve.wait_ge(cv_step, base)
            w = COLS["conv"][0] + 3 * c
            dve.tensor_tensor(cu[:, 2:], ps[:, b[0], :], cy[:, :], ALU.mult).then_inc(cv_step, 1)
            dve.wait_ge(cv_step, base + 1)
            dve.tensor_scalar(cy[:, :], cu[:, 2:], cols[:, w + 2:w + 3], None, ALU.mult).then_inc(cv_step, 1)
            for n in (1, 0):
                dve.wait_ge(cv_step, base + 3 - n)
                dve.scalar_tensor_tensor(cy[:, :], cu[:, n:n + T], cols[:, w + n:w + n + 1], cy[:, :], ALU.mult, ALU.add).then_inc(cv_step, 1)
            dve.wait_ge(cv_step, base + 4)
            dve.tensor_tensor(cy[:, :], cy[:, :], ps[:, b[1], :], ALU.mult).then_inc(cv_step, 2)

        def conv_low_dve(dve, c):
            dve.wait_ge(cv_h, c + 1)
            dve.tensor_tensor(ocL[:, c, :], cy[:, :], ocH[:, c, :].bitcast(F32), ALU.subtract).then_inc(cv_step, 1)

        def mix_dve(dve):
            norm_gain(dve, 1, col("norm_w", 8, 8), mod[:, 32:40])
            norm_dve(dve, 1, mod[:, 24:32])
            acc_clear(dve, 2)
            n = [0]

            def step(ins):
                ins.then_inc(tb_step, 1)
                n[0] += 1
                dve.wait_ge(tb_step, n[0])

            dve.wait_ge(s_pos, 16)
            step(dve.memset(cu[:, 0:2], 0.0))
            step(dve.tensor_copy(cosT[:, :], sinT[:, :].bitcast(I32)))
            step(dve.tensor_scalar(cosT[:, :], cosT[:, :], col("inv_freq"), None, ALU.mult))
            step(dve.tensor_scalar(sinT[:, :], cosT[:, :], 1.0 / (2 * np.pi), 12582912.0, ALU.mult, ALU.add))
            step(dve.tensor_scalar(sinT[:, :], sinT[:, :], -12582912.0, None, ALU.add))
            c1 = 6.28125
            c2 = float(np.float32(np.floor((2 * np.pi - c1) * 2 ** 20) / 2 ** 20))
            for c in (c1, c2, 2 * np.pi - c1 - c2):
                step(dve.scalar_tensor_tensor(cosT[:, :], sinT[:, :], -c, cosT[:, :], ALU.mult, ALU.add))
            step(dve.tensor_scalar(cosT[:, :], cosT[:, :], 3.1415925, -3.1415925, ALU.min, ALU.max))
            dve.wait_ge(tb_sin, 2)
            step(dve.tensor_scalar(cosT[:, :], cosT[:, :], -1.0, np.pi / 2, ALU.mult, ALU.add))
            for i in range(4):
                split_lo(dve, B0 + i + LEAD)
            split_lo(dve, B_CONV[0] + LEAD)
            for i in range(4):
                dve.wait_ge(c_rs, (2, 2, 4, 6)[i])
                w = (col("qa", 0), col("qa", 1), col("kva"), col("kr"))[i]
                dve.scalar_tensor_tensor(c32[:, i, :], c32[:, i, :], w, crs[:, (0, 0, 1, 0)[i], :], ALU.mult, ALU.mult).then_inc(c_n, 1)
            for i in range(3):
                dve.wait_ge(c_h, i + 1)
                dve.tensor_tensor(cL[:, i, :], c32[:, i, :], cH[:, i, :].bitcast(F32), ALU.subtract).then_inc(c_l, 1)
            dve.wait_ge(tb_sin, 3)
            dve.wait_ge(kr_rot, 1)
            dve.tensor_tensor(sq[:, :], ps[:, 2, :], sinT[:, :], ALU.mult).then_inc(kr_step, 1)
            dve.tensor_tensor(c32[:, 3, :], c32[:, 3, :], cosT[:, :], ALU.mult).then_inc(kr_step, 1)
            dve.wait_ge(kr_step, 2)
            dve.tensor_tensor(c32[:, 3, :], c32[:, 3, :], sq[:, :], ALU.add).then_inc(kr_step, 1)
            dve.wait_ge(kr_step, 3)
            for par in range(2):
                r = slice(64 * (1 - par), 64 * (1 - par) + 64)
                dve.tensor_copy(kT[r, :, :].rearrange("p (m two) t -> p m two t", two=2)[:, :, par, :],
                                c32[r, 3, :].unsqueeze(1).broadcast_to([64, 4, T])).then_inc(kr_step, 1)
            split_lo(dve, B_CONV[0] + 1 + LEAD)
            split_lo(dve, B_CONV[0] + 2 + LEAD)
            conv_dve(dve, 0)
            conv_low_dve(dve, 0)
            for t in range(13):
                if t < 12:
                    dve.wait_ge(up_rs, 2 * t + 2)
                    if t < 8:
                        dve.scalar_tensor_tensor(qT[:, t, :], ps[:, t % 3, :], col(("qe", "qo")[t % 2]), crs[:, t % 2, :],
                                                 ALU.mult, ALU.mult).then_inc(up_n, 1)
                    else:
                        for par in range(2):
                            r = slice(64 * par, 64 * par + 64)
                            last = dve.scalar_tensor_tensor(kT[r, 2 * (t - 8) + par, :], ps[r, t % 3, :], col("kn")[r, :],
                                                            crs[r, t % 2, :], ALU.mult, ALU.mult)
                        last.then_inc(up_n, 1)
                if t == 3:
                    split_lo(dve, B_UP + LEAD)
                if t == 8:
                    split_lo(dve, B_UP + 1 + LEAD)
                if 1 <= t <= 8:
                    h = t - 1
                    r = rows(h)
                    dve.wait_ge(up_rot, h + 1)
                    if h:
                        dve.wait_ge(up_r, 3 * h)
                    dve.tensor_tensor(sq[r, :], ps[r, 5 + h % 2, :], sinT[r, :], ALU.mult).then_inc(up_r, 1)
                    dve.tensor_tensor(qT[r, h, :], qT[r, h, :], cosT[r, :], ALU.mult).then_inc(up_r, 1)
                    dve.wait_ge(up_r, 3 * h + 2)
                    dve.tensor_tensor(qT[r, h, :], qT[r, h, :], sq[r, :], ALU.add).then_inc(up_r, 1)
            split_lo(dve, B_UP + 2 + LEAD)
            for h in range(HEADS):
                b4 = h % 2
                if h >= 2:
                    dve.wait_ge(at_p, 5 * (h - 1))
                for n_, i in enumerate(S_ORDER):
                    b, c0 = S_BANK[i]
                    dve.wait_ge(at_s, 4 * h + S_NEED[n_])
                    dg = ps[:, b, c0 + i * P:c0 + (i + 1) * P]
                    dve.tensor_tensor(dg, dg, const("causal"), ALU.add).then_inc(at_m, 1)
                    dve.wait_ge(at_m, 9 * h + 2 * n_ + 1)
                    dve.tensor_reduce(st[:, b4, i:i + 1], ps[:, b, c0:c0 + (i + 1) * P], AX.X, ALU.max).then_inc(at_m, 1)
                dve.wait_ge(at_m, 9 * h + 8)
                dve.tensor_scalar(st[:, b4, 4:8], st[:, b4, 0:4], -ATT_SCALE, None, ALU.mult).then_inc(at_m, 1)
                dve.wait_ge(at_e, 4 * h + 4)
                dve.reciprocal(st[:, b4, 12:16], st[:, b4, 8:12]).then_inc(at_p, 1)
                dve.wait_ge(at_p, 5 * h + 1)
                for i in range(4):
                    pi = pr[:, b4, POFF[i]:POFF[i] + (i + 1) * P]
                    dve.tensor_scalar(pi, pi, st[:, b4, 12 + i:13 + i], None, ALU.mult).then_inc(at_p, 1)
                split_lo(dve, B_CONV[1] + h + LEAD)
                if h % 3 == 2:
                    conv_dve(dve, 1 + h // 3)
                if h % 2 == 1:
                    dve.wait_ge(at_h, h // 2 + 1)
                    dve.tensor_tensor(oaL[:, h // 2, :], ps[:, 7, :], oaH[:, h // 2, :].bitcast(F32), ALU.subtract).then_inc(at_l, 1)
                if h % 3 == 2:
                    conv_low_dve(dve, 1 + h // 3)
            split_lo(dve, B_CONV[1] + 8 + LEAD)
            conv_dve(dve, 3)
            conv_low_dve(dve, 3)
            with dve.Fori(0, 4) as g:
                for t in range(2):
                    o = at(t, g, 2)
                    for u in range(3):
                        split_lo(dve, B_GB + 3 * t + u + LEAD, g, 6)
                    wait_slot(dve, B_GB + 3 * t + 2, g, 6)
                    for u in range(2):
                        dve.wait_ge(gb_s, at(2 * t + u + 1, g, 4) if u == 0 else at(2 * t + 2, g, 4))
                        dve.tensor_tensor(sg[:, u, :], ps[:, 4 * t + 2 + u, :], sg[:, u, :], ALU.mult).then_inc(gb_m, 1)
                    dve.wait_ge(gb_m, 3 * o + 8)
                    dve.wait_ge(gb_l, o + 1)
                    dve.tensor_tensor(cy[:, :], sg[:, 0, :], sg[:, 1, :], ALU.add).then_inc(gb_m, 1)
                    dve.wait_ge(gb_h, o + 1)
                    dve.tensor_tensor(pick(mL, o), cy[:, :], pick(mH, o).bitcast(F32), ALU.subtract).then_inc(gb_l, 1)
            for o in range(KD):
                split_lo(dve, B_OUT + o + LEAD)
                wait_slot(dve, B_OUT + o)
                dve.scalar_tensor_tensor(xT[:, o, :], ps[:, o, :], mod[:, 40 + o:41 + o], xT[:, o, :], ALU.mult, ALU.add).then_inc(resid, 1)
                acc_add(dve, 2, o)

        def mix_pool(pool):
            pool.wait_ge(rs_step, 4)
            pool.dma_start(sinT[:, :].bitcast(I32), posd.partition_broadcast(P)).then_inc(s_pos, 16)

        W = T + TC
        NL = len(LEVELS)
        F_AT = [2 * W - (2 * W >> l) for l in range(NL + 1)]
        with ExitStack() as ph:
            hcH = sb("hcH", [P, KD, TC], F32R, ph)
            hcL = sb("hcL", [P, KD, TC], F32R, ph)
            mask32 = sb("mask32", [P, NL + 1, P], I32, ph)
            mask = sb("mask", [P, NL + 1, P], U8, ph)
            lbc = sb("lbc", [P, 3, 32], F32, ph)
            sg_f = sb("sg_f", [P, 2, W], F32, ph)
            XL = sb("XL", [P, 2, W], F32, ph)
            XR = sb("XR", [P, 2, W], F32, ph)
            fp = sb("fp", [P, 2, 2 * W], F32, ph)
            kd = sb("kd", [P, T], F32, ph)
            KQ = sb("KQ", [P, 2, 2, T], F32, ph)
            scT = sb("scT", [P, T], F32, ph)
            khT = sb("khT", [P, 2, 5, P], F32, ph)
            stS = sb("stS", [P, 2, 4, P], F32, ph)
            q32 = sb("q32", [P, T], F32, ph)
            v32 = sb("v32", [P, W], F32, ph)
            vt6 = sb("vt6", [P, 6, P], F32, ph)
            zs = sb("zs", [P, T], F32, ph)
            y32 = sb("y32", [P, T], F32, ph)
            yH = sb("yH", [P, T], F32R, ph)
            yL = sb("yL", [P, T], F32R, ph)
        with ExitStack() as ph:
            sb("hole_h", [P, 2 * KD * TC], F32, ph)
            sb("hole_m", [P, 2 * (NL + 1) * P], I32, ph)
            sb("hole_l", [P, 96], F32, ph)
            cin = sb("cin", [P, 2, D], F32, ph)
            cxT = sb("cxT", [P, KD, TC], F32, ph)

        s_ctx = sem("s_ctx")
        s_mask = sem("s_mask")
        cx_t = sem("cx_t")
        cx_c = sem("cx_c")
        lb_step = sem("lb_step")
        lb_e = sem("lb_e")
        h_clear = sem("h_clear")
        h_sg = sem("h_sg")
        h_qs = sem("h_qs")
        h_q = sem("h_q")
        h_v = sem("h_v")
        h_vt = sem("h_vt")
        h_vc = sem("h_vc")
        h_zs = sem("h_zs")
        h_z = sem("h_z")
        h_in = sem("h_in")
        h_q0 = sem("h_q0")
        h_kd = sem("h_kd")
        h_mg = sem("h_mg")
        h_xl = sem("h_xl")
        h_xr = sem("h_xr")
        h_xc = sem("h_xc")
        h_f = sem("h_f")
        h_sc = sem("h_sc")
        h_pl = sem("h_pl")
        h_kt = sem("h_kt")
        h_kc = sem("h_kc")
        h_u = sem("h_u")
        h_st = sem("h_st")
        h_o = sem("h_o")
        h_os = sem("h_os")
        h_ms = sem("h_ms")
        h_rs = sem("h_rs")
        h_y = sem("h_y")
        h_yh = sem("h_yh")
        h_yl = sem("h_yl")
        h_w = sem("h_w")

        HG_R = 24 + 2

        def hcol(t, i, dr, h):
            v = t[:, i, 16 * dr:16 * dr + 16]
            return v[:, h:h + 1] if isinstance(h, int) else v[:, bass.ds(h, 1)]

        def halves(t, lv):
            v = t.rearrange("p d (b t) -> p d b t", t=2 * lv)
            return v[:, :, :, 0:lv], v[:, :, :, lv:2 * lv]

        def blocks_of(l, lo, n, side):
            w = 1 << l
            v = fp[:, :, F_AT[l] + lo // w:F_AT[l] + (lo + n) // w].rearrange("p d (b s) -> p d b s", s=2)
            return v[:, :, :, side:side + 1]

        def spread(v, w):
            return v.broadcast_to([P, v.shape[1], v.shape[2], w])

        def after(eng, s, v):
            if not isinstance(v, int) or v > 0:
                eng.wait_ge(s, v)

        def hg_slots(i):
            if isinstance(i, int):
                if i == 0:
                    return S_HG + 5, 0, {"f0": 0, "f1": 1, "q": 2, "z": 3, "v": 4}
                if i == HG - 1:
                    return S_HG + 4 + 6 * i, 0, {"w": 0}
            return S_HG + 4, i, {"f0": 0, "f1": 1, "w": 2, "q": 3, "z": 4, "v": 5}

        def context_pe(pe, lo, hi):
            for k in range(lo, hi):
                if k >= 4:
                    pe.wait_ge(sq_done, 32 + k - 3)
                for a in range(2):
                    last = pe.transpose(ps[:, 4 + k % 4, a * P:(a + 1) * P], cin[:, a, k * P:(k + 1) * P], const("ident"))
                last.then_inc(cx_t, 1)

        def context_act(act):
            for k in range(KD):
                act.wait_ge(cx_t, k + 1)
                act.activation(cxT[:, k, :], ps[:, 4 + k % 4, 0:TC], ACT.Copy).then_inc(cx_c, 1)
                square(act, 4, k, ps[:, 4 + k % 4, 0:TC], TC)
            norm_act(act, 4, 6, mod[:, 120:128], TC, hcH)

        def context_dve(dve):
            acc_clear(dve, 4)
            for k in range(KD):
                acc_add(dve, 4, k, TC)
            norm_gain(dve, 4, col("norm_g2", 0, 8), mod[:, 128:136])
            norm_dve(dve, 4, mod[:, 120:128], TC, hcH, hcL, cxT)


        def lat_pe(pe, s, r, bank):
            return gemm(pe, ps[:, bank, :], s, r, 6, hH, hL)

        def con_pe(pe, s, bank, half):
            j = s % RING
            for k in range(KD):
                w = slice(k * P, (k + 1) * P)
                last = products(pe, ps[:, bank, TC * half:TC * half + TC], wh[:, j, w], wl[:, j, w], hcH[:, k, :], hcL[:, k, :],
                                k == 0, k == KD - 1, skip_group_check=True)
            return last

        def value_pe(pe, n):
            pe.wait_ge(h_v, at(2, n, 2))
            for bank, at_, tiles in ((5, 0, 4), (3, T, 2)):
                for c in range(tiles):
                    last = pe.transpose(ps[:, bank, c * P:(c + 1) * P], v32[:, at_ + c * P:at_ + (c + 1) * P], const("ident"))
                last.then_inc(h_vt, 1)

        def scores_hg(pe, n, j):
            if j == 0:
                pe.wait_ge(h_kd, n + 1)
                after(pe, h_rs, 2 * n)
            else:
                pe.wait_ge(h_mg, at(3 * j, n, 3 * NL))
                if j == 1:
                    after(pe, h_y, 2 * n - 1)
            if j >= 2:
                pe.wait_ge(h_pl, at(j - 1, n, NL + 1))
            kt_, qt_ = (kd[:, :], q32[:, :]) if j == 0 else (KQ[:, (j - 1) % 2, 0, :], KQ[:, (j - 1) % 2, 1, :])
            for c in range(4):
                r = slice(c * P, (c + 1) * P)
                last = pe.matmul(ps[:, 6 + j % 2, r], kt_[:, r], qt_[:, r], start=True, stop=True, skip_group_check=True)
            last.then_inc(h_sc, 1)

        def ms_pe(pe, n):
            pe.wait_ge(h_os, n + 1)
            pe.wait_ge(h_st, at(8, n, 8))
            pe.matmul(ps[:, 6, :], const("ones"), sq[:, :], start=True, stop=True).then_inc(h_ms, 1)

        OUT_BANKS = (0, 3, 5)

        def out_pe(pe, s, r, n):
            slot_ready(pe, s, r, 6)
            pe.wait_ge(h_yl, n + 1)
            j = s % RING
            for o in range(KD):
                if o >= 3:
                    pe.wait_ge(resid, at(HG_R + o - 2, n, 8))
                w, b = slice(o * P, (o + 1) * P), OUT_BANKS[o % 3]
                products(pe, ps[:, b, :], wh[:, j, w], wl[:, j, w], yH[:, :], yL[:, :], True, True).then_inc(h_w, 1)
            pe.drain().then_inc(slot_done, 1)

        def step_pe(pe, i, more, prev):
            s, r, a = hg_slots(i)
            if more:
                lat_pe(pe, s + a["f0"], r, 0)
            if prev:
                ms_pe(pe, i - 1)
            if more:
                con_pe(pe, s + a["f0"], 2, 0).then_inc(slot_done, 1)
            if more:
                lat_pe(pe, s + a["f1"], r, 1)
            scores_hg(pe, i, 0)
            value_pe(pe, i)
            scores_hg(pe, i, 1)
            if more:
                pe.wait_ge(h_sg, at(6, i, 4))
                con_pe(pe, s + a["f1"], 2, 1).then_inc(slot_done, 1)
            scores_hg(pe, i, 2)
            if prev:
                if more:
                    pe.wait_ge(h_sg, at(6, i, 4))
                pe.wait_ge(h_vc, at(2, i, 2))
                out_pe(pe, s + a["w"], r, i - 1)
            scores_hg(pe, i, 3)
            if more:
                pe.wait_ge(h_vc, at(2, i, 2))
                pe.wait_ge(resid, at(HG_R, i, 8))
                lat_pe(pe, s + a["q"], r, 3).then_inc(slot_done, 1)
            scores_hg(pe, i, 4)
            if more:
                pe.wait_ge(h_z, i + 1)
                slot_ready(pe, s + a["z"], r, 6)
                z_j = (s + a["z"]) % RING
            for part in range(4):
                if more:
                    for k in (2 * part, 2 * part + 1):
                        w = slice(k * P, (k + 1) * P)
                        last = products(pe, ps[:, 4, :], wh[:, z_j, w], wl[:, z_j, w], hH[:, k, :], hL[:, k, :], k == 0, k == KD - 1)
                    if part == 3:
                        last.then_inc(slot_done, 1)
                if part < 3:
                    scores_hg(pe, i, 5 + part)
            pe.wait_ge(resid, at(HG_R, i, 8))
            if more:
                pe.wait_ge(h_sg, at(8, i, 4))
            pe.wait_ge(h_xl, at(NL, i, NL))
            for c in range(3):
                last = pe.transpose(ps[:, 0, c * P:(c + 1) * P], XL[:, 0, c * P:(c + 1) * P], const("ident"))
            last.then_inc(h_kt, 1)
            pe.wait_ge(h_xr, at(NL, i, NL))
            for c in range(3):
                last = pe.transpose(ps[:, 1, c * P:(c + 1) * P], XR[:, 1, (c + 1) * P:(c + 2) * P], const("ident"))
            last.then_inc(h_kt, 1)
            pe.wait_ge(h_xc, at(2 * NL + 2, i, 2 * NL + 2))
            for c in range(4):
                src = (XL[:, 0, T:], XR[:, 1, T:])[c // 2][:, (c % 2) * P:(c % 2 + 1) * P]
                last = pe.transpose(ps[:, 2, c * P:(c + 1) * P], src, const("ident"))
            last.then_inc(h_kt, 1)
            if more:
                pe.wait_ge(resid, at(HG_R, i, 8))
                lat_pe(pe, s + a["v"], r, 5)
            pe.wait_ge(h_kc, at(3, i, 3))
            pe.wait_ge(h_pl, at(NL + 1, i, NL + 1))
            for d in range(2):
                for c in range(2):
                    pe.matmul(ps[:, 6 + d, 0:P], khT[:, d, 3 + c, :], vt6[:, 4 + c, :], start=(c == 0), stop=(c == 1), skip_group_check=True)
                for c in range(3):
                    last = pe.matmul(ps[:, 6 + d, (c + 1) * P:(c + 2) * P], khT[:, d, c, :], vt6[:, c + d, :], start=True, stop=True, skip_group_check=True)
                last.then_inc(h_u, 1)
            if more:
                pe.wait_ge(h_q, at(2, i, 1))
                con_pe(pe, s + a["v"], 3, 0).then_inc(slot_done, 1)
            pe.wait_ge(h_st, at(8, i, 8))
            for c in range(4):
                r_ = slice(c * P, (c + 1) * P)
                pe.matmul(ps[:, 7, r_], vt6[:, c, :], scT[:, r_], start=(c == 0), stop=False, skip_group_check=True)
            for d in range(2):
                for c in range(4):
                    r_ = slice(c * P, (c + 1) * P)
                    last = pe.matmul(ps[:, 7, r_], stS[:, d, c, :], (XR[:, 0, r_], XL[:, 1, r_])[d], start=False, stop=(d == 1 and c == 3), skip_group_check=True)
            last.then_inc(h_o, 1)

        def hg_pe(pe):
            norm_pe(pe, 3, 2)
            pe.wait_ge(ada_r, 51)
            pe.wait_ge(s_ctx, 16)
            context_pe(pe, 0, 4)
            s = S_HG
            gemm(pe, ps[:, 0, :], s, 0, 0, hH, hL, 24)
            context_pe(pe, 4, KD)
            lat_pe(pe, s + 1, 0, 1)
            norm_pe(pe, 4, 6, TC)
            lat_pe(pe, s + 2, 0, 3)
            pe.wait_ge(nl_done, 40)
            con_pe(pe, s, 2, 0).then_inc(slot_done, 1)
            pe.wait_ge(h_sg, 2)
            con_pe(pe, s + 1, 2, 1).then_inc(slot_done, 1)
            pe.drain().then_inc(slot_done, 1)
            lat_pe(pe, s + 3, 0, 4).then_inc(slot_done, 1)
            lat_pe(pe, s + 4, 0, 5)
            pe.wait_ge(h_q, 1)
            con_pe(pe, s + 4, 3, 0).then_inc(slot_done, 1)
            pe.wait_ge(h_clear, 4)
            step_pe(pe, 0, True, False)
            with pe.Fori(1, HG - 1) as i:
                step_pe(pe, i, True, True)
            step_pe(pe, HG - 1, False, True)
            ms_pe(pe, HG - 1)
            out_pe(pe, S_HG + 6 * HG - 1, 0, HG - 1)

        def gates_act(act, s, r, n, d):
            wait_slot(act, s, r, 6)
            if d == 0:
                after(act, h_in, 4 * n)
            act.activation(sg_f[:, d, 0:T], ps[:, d, :], ACT.Sigmoid).then_inc(h_sg, 1)
            act.activation(sg_f[:, d, T:], ps[:, 2, TC * d:TC * d + TC], ACT.Sigmoid).then_inc(h_sg, 1)

        def query_act(act, s, r, n):
            wait_slot(act, s, r, 6)
            after(act, h_q0, 2 * n)
            after(act, h_sc, (NL + 1) * n - NL)
            act.activation(q32[:, :], ps[:, 3, :], ACT.Sigmoid).then_inc(h_qs, 1)

        def z_act(act, n):
            after(act, h_y, 2 * n)
            act.activation(zs[:, :], ps[:, 4, :], ACT.Sigmoid).then_inc(h_zs, 1)

        def value_act(act, s, r, n):
            wait_slot(act, s, r, 6)
            after(act, h_vt, 2 * n)
            act.activation(v32[:, 0:T], ps[:, 5, :], ACT.Copy).then_inc(h_v, 1)
            act.activation(v32[:, T:], ps[:, 3, 0:TC], ACT.Copy).then_inc(h_v, 1)

        def value_copy_act(act, n):
            after(act, h_o, n)
            act.wait_ge(h_vt, at(1, n, 2))
            act.activation(vt6[:, 0:4, :], ps[:, 5, :].rearrange("p (c v) -> p c v", v=P), ACT.Copy).then_inc(h_vc, 1)
            act.wait_ge(h_vt, at(2, n, 2))
            act.activation(vt6[:, 4:6, :], ps[:, 3, 0:TC].rearrange("p (c v) -> p c v", v=P), ACT.Copy).then_inc(h_vc, 1)

        def merge_act(act, n, l):
            lv = 1 << l
            if l == 0:
                act.wait_ge(h_q0, at(2, n, 2))
                after(act, h_sc, (NL + 1) * n)
            else:
                act.wait_ge(h_xl, at(l, n, NL))
                act.wait_ge(h_xr, at(l, n, NL))
            if l >= 2:
                act.wait_ge(h_sc, at(l, n, NL + 1))
            left, right = halves(KQ[:, l % 2, :, :], lv)
            act.activation(left, halves(XL[:, :, 0:T], lv)[0], ACT.Copy).then_inc(h_mg, 1)
            act.activation(right[:, 0], halves(XR[:, :, 0:T], lv)[1][:, 1], ACT.Copy).then_inc(h_mg, 1)
            act.activation(right[:, 1], halves(XR[:, :, 0:T], lv)[1][:, 0], ACT.Copy).then_inc(h_mg, 1)

        def rms_act(act, n):
            act.preload_act_table_set(EXP_LN)
            act.wait_ge(h_ms, n + 2)
            act.activation(rs[:, :], ps[:, 6, :], ACT.Ln, bias=epsc[:, :], scale=1.0 / P).then_inc(h_rs, 1)
            act.wait_ge(h_rs, at(1, n, 2))
            act.activation(rs[:, :], rs[:, :], ACT.Exp, scale=-0.5).then_inc(h_rs, 1)

        def y_act(act, n):
            act.wait_ge(h_y, at(2, n, 2))
            act.wait_ge(resid, at(HG_R, n, 8))
            act.activation(yH[:, :], y32[:, :], ACT.Copy).then_inc(h_yh, 1)

        def step_act(act, i, more, prev):
            s, r, a = hg_slots(i)

            def split(name):
                if name in a:
                    split_hi(act, s + a[name] + LEAD, r, 6)

            split("f0")
            if prev:
                act.wait_ge(h_o, i)
                act.wait_ge(h_ms, i)
                act.activation(sq[:, :], ps[:, 7, :], ACT.Square).then_inc(h_os, 1)
            merge_act(act, i, 0)
            if more:
                gates_act(act, s + a["f0"], r, i + 1, 0)
            if prev:
                rms_act(act, i - 1)
            split("f1")
            merge_act(act, i, 1)
            if prev:
                y_act(act, i - 1)
            z_act(act, i)
            value_copy_act(act, i)
            merge_act(act, i, 2)
            if more:
                gates_act(act, s + a["f1"], r, i + 1, 1)
            merge_act(act, i, 3)
            split("w")
            merge_act(act, i, 4)
            if more:
                split("q")
                query_act(act, s + a["q"], r, i + 1)
            merge_act(act, i, 5)
            split("z")
            merge_act(act, i, 6)
            for c in range(3):
                act.wait_ge(h_kt, at(c + 1, i, 3))
                if c == 0:
                    after(act, h_u, 2 * i)
                dst = khT[:, c, 0:3, :] if c < 2 else khT[:, :, 3:5, :]
                src = ps[:, c, 0:3 * P].rearrange("p (c v) -> p c v", v=P) if c < 2 else ps[:, 2, :].rearrange("p (d c v) -> p d c v", d=2, v=P)
                act.activation(dst, src, ACT.Copy).then_inc(h_kc, 1)
            split("v")
            if more:
                value_act(act, s + a["v"], r, i + 1)

        def hg_act(act):
            norm_act(act, 3, 2, mod[:, 72:80])
            split_hi(act, S_HG + LEAD)
            context_act(act)
            act.wait_ge(lb_step, 2)
            act.activation(lbc[:, 0:2, :], lbc[:, 0:2, :], ACT.Exp).then_inc(lb_e, 1)
            s = S_HG
            for d in range(2):
                if d:
                    split_hi(act, s + d + LEAD)
                gates_act(act, s + d, 0, 0, d)
            split_hi(act, s + 2 + LEAD)
            query_act(act, s + 2, 0, 0)
            split_hi(act, s + 3 + LEAD)
            split_hi(act, s + 4 + LEAD)
            value_act(act, s + 4, 0, 0)
            step_act(act, 0, True, False)
            with act.Fori(1, HG - 1) as i:
                step_act(act, i, True, True)
            step_act(act, HG - 1, False, True)
            last = HG - 1
            act.wait_ge(h_o, HG)
            act.wait_ge(h_ms, last + 1)
            act.activation(sq[:, :], ps[:, 7, :], ACT.Square).then_inc(h_os, 1)
            rms_act(act, last)
            split_hi(act, S_HG + 6 * HG - 1 + LEAD)
            y_act(act, last)
            for k in range(KD):
                act.wait_ge(resid, HG_R + 8 * last + k + 1)
                square(act, 5, k, xT[:, k, :])

        def init_dve(dve, n):
            dve.wait_ge(h_sg, at(4, n, 4))
            after(dve, h_o, n)
            after(dve, h_xc, (2 * NL + 2) * n)
            for d in range(2):
                dve.tensor_scalar((XL[:, 0, :], XR[:, 1, :])[d], sg_f[:, d, :], hcol(lbc, 2, d, n), hcol(lbc, 1, d, n), ALU.mult, ALU.add).then_inc(h_in, 1)
                dve.tensor_scalar(fp[:, d, 0:W], sg_f[:, d, :], hcol(lbc, 1, d, n), hcol(lbc, 0, d, n), ALU.mult, ALU.add).then_inc(h_in, 1)
            dve.wait_ge(h_in, at(4, n, 4))
            dve.wait_ge(h_q, n + 1)
            dve.tensor_tensor(kd[:, :], XL[:, 0, 0:T], XR[:, 1, 0:T], ALU.add).then_inc(h_kd, 1)
            dve.tensor_tensor(XR[:, 0, 0:T], q32[:, :], fp[:, 0, 0:T], ALU.mult).then_inc(h_q0, 1)
            dve.tensor_tensor(XL[:, 1, 0:T], q32[:, :], fp[:, 1, 0:T], ALU.mult).then_inc(h_q0, 1)

        def query_dve(dve, n):
            dve.wait_ge(h_qs, n + 1)
            dve.tensor_tensor(q32[:, :], q32[:, :], ps[:, 3, :], ALU.mult).then_inc(h_q, 1)

        def level_dve(dve, n, l):
            a, w = F_AT[l], W >> l
            v = fp[:, :, a:a + w].rearrange("p d (b s) -> p d b s", s=2)
            if l:
                dve.wait_ge(h_f, at(l, n, NL))
            dve.tensor_tensor(fp[:, :, a + w:a + w + w // 2], v[:, :, :, 0], v[:, :, :, 1], ALU.mult).then_inc(h_f, 1)
            lv = 1 << l
            left = halves(XL[:, :, 0:T], lv)[0]
            if l:
                dve.wait_ge(h_xl, at(l, n, NL))
            dve.wait_ge(h_mg, at(3 * l + 3, n, 3 * NL))
            dve.tensor_tensor(left, left, spread(blocks_of(l, 0, T, 1), lv), ALU.mult).then_inc(h_xl, 1)

        def place(dve, n, j):
            dve.wait_ge(h_sc, at(j + 1, n, NL + 1))
            if j:
                dve.wait_ge(h_pl, at(j, n, NL + 1))
            dve.sem_inc(paced_dve, 1)
            dve.copy_predicated(scT[:, :].rearrange("p (c t) -> p c t", t=P),
                                mask[:, j, :].unsqueeze(1).broadcast_to([P, 4, P]),
                                ps[:, 6 + j % 2, :].rearrange("p (c t) -> p c t", t=P)).then_inc(h_pl, 1)

        def states_dve(dve, n):
            for d in range(2):
                dve.wait_ge(h_u, at(d + 1, n, 2))
                dve.tensor_copy(stS[:, d, 3 * d, :], ps[:, 6 + d, 0:P]).then_inc(h_st, 1)
            for c in range(3):
                for d in range(2):
                    i = (c, 3 - c)[d]
                    u = (c, 2 - c)[d]
                    nxt = i + 1 if d == 0 else i - 1
                    e = F_AT[NL] + i
                    dve.wait_ge(h_st, at(2 * c + d + 1, n, 8))
                    dve.scalar_tensor_tensor(stS[:, d, nxt, :], stS[:, d, i, :], fp[:, d, e:e + 1],
                                             ps[:, 6 + d, (u + 1) * P:(u + 2) * P], ALU.mult, ALU.add).then_inc(h_st, 1)

        def y_dve(dve, n):
            dve.wait_ge(h_rs, at(2, n, 2))
            dve.wait_ge(resid, at(HG_R, n, 8))
            dve.tensor_tensor(y32[:, :], ps[:, 7, :], rs[:, :], ALU.mult).then_inc(h_y, 1)
            dve.wait_ge(h_y, at(1, n, 2))
            dve.scalar_tensor_tensor(y32[:, :], y32[:, :], col("hg_norm"), zs[:, :], ALU.mult, ALU.mult).then_inc(h_y, 1)

        def yl_dve(dve, n):
            dve.wait_ge(h_yh, n + 1)
            dve.tensor_tensor(yL[:, :], y32[:, :], yH[:, :].bitcast(F32), ALU.subtract).then_inc(h_yl, 1)

        def z_dve(dve, n):
            dve.wait_ge(h_zs, n + 1)
            dve.tensor_tensor(zs[:, :], ps[:, 4, :], zs[:, :], ALU.mult).then_inc(h_z, 1)

        def out_dve(dve, n, o):
            dve.wait_ge(h_w, at(o + 1, n, 8))
            dve.scalar_tensor_tensor(xT[:, o, :], ps[:, OUT_BANKS[o % 3], :], mod[:, 88 + o:89 + o], xT[:, o, :],
                                     ALU.mult, ALU.add).then_inc(resid, 1)

        def step_dve(dve, i, more, prev):
            s, r, a = hg_slots(i)

            def split(name):
                if name in a:
                    split_lo(dve, s + a[name] + LEAD, r, 6)

            init_dve(dve, i)
            split("f0")
            level_dve(dve, i, 0)
            if prev:
                y_dve(dve, i - 1)
            place(dve, i, 0)
            split("f1")
            level_dve(dve, i, 1)
            place(dve, i, 1)
            if prev:
                yl_dve(dve, i - 1)
            z_dve(dve, i)
            level_dve(dve, i, 2)
            place(dve, i, 2)
            if prev:
                for o in range(5):
                    out_dve(dve, i - 1, o)
            level_dve(dve, i, 3)
            if prev:
                for o in range(5, KD):
                    out_dve(dve, i - 1, o)
            split("w")
            place(dve, i, 3)
            level_dve(dve, i, 4)
            split("q")
            place(dve, i, 4)
            if more:
                query_dve(dve, i + 1)
            level_dve(dve, i, 5)
            place(dve, i, 5)
            split("z")
            level_dve(dve, i, 6)
            place(dve, i, 6)
            place(dve, i, 7)
            split("v")
            states_dve(dve, i)

        def hg_dve(dve):
            dve.wait_ge(ada_r, 51)
            norm_gain(dve, 3, col("norm_g2", 0, 8), mod[:, 80:88])
            norm_dve(dve, 3, mod[:, 72:80])
            split_lo(dve, S_HG + LEAD)
            context_dve(dve)
            acc_clear(dve, 5)
            lb = col("lb", 0, 64)
            dve.tensor_tensor(lbc[:, 2, :], lb[:, 0:32], lb[:, 32:64], ALU.max).then_inc(lb_step, 1)
            dve.wait_ge(lb_step, 1)
            dve.tensor_tensor(lbc[:, 0:2, :], lb.rearrange("p (r n) -> p r n", r=2),
                              lbc[:, 2, :].unsqueeze(1).broadcast_to([P, 2, 32]), ALU.subtract).then_inc(lb_step, 1)
            dve.wait_ge(lb_e, 1)
            dve.tensor_tensor(lbc[:, 2, :], lbc[:, 0, :], lbc[:, 1, :], ALU.add).then_inc(lb_step, 1)
            dve.wait_ge(lb_step, 3)
            dve.reciprocal(lbc[:, 2, :], lbc[:, 2, :]).then_inc(lb_step, 1)
            dve.wait_ge(lb_step, 4)
            dve.tensor_tensor(lbc[:, 0, :], lbc[:, 0, :], lbc[:, 2, :], ALU.mult).then_inc(lb_step, 1)
            dve.wait_ge(lb_step, 5)
            dve.tensor_scalar(lbc[:, 1, :], lbc[:, 0, :], -1.0, 1.0, ALU.mult, ALU.add).then_inc(lb_step, 1)
            dve.tensor_scalar(lbc[:, 2, :], lbc[:, 0, :], 1.0, -1.0, ALU.mult, ALU.add).then_inc(lb_step, 1)
            dve.wait_ge(lb_step, 7)
            dve.memset(scT[:, :], 0.0).then_inc(h_clear, 1)
            dve.wait_ge(s_mask, 16)
            dve.tensor_copy(mask[:, :, :], mask32[:, :, :]).then_inc(h_clear, 1)
            dve.memset(XL[:, 1, T:], 0.0).then_inc(h_clear, 1)
            dve.memset(XR[:, 0, T:], 0.0).then_inc(h_clear, 1)
            dve.wait_ge(h_clear, 4)
            s = S_HG
            split_lo(dve, s + 1 + LEAD)
            split_lo(dve, s + 2 + LEAD)
            query_dve(dve, 0)
            split_lo(dve, s + 3 + LEAD)
            split_lo(dve, s + 4 + LEAD)
            step_dve(dve, 0, True, False)
            with dve.Fori(1, HG - 1) as i:
                step_dve(dve, i, True, True)
            step_dve(dve, HG - 1, False, True)
            last = HG - 1
            y_dve(dve, last)
            split_lo(dve, S_HG + 6 * HG - 1 + LEAD)
            yl_dve(dve, last)
            for o in range(KD):
                out_dve(dve, last, o)
                if o:
                    acc_add(dve, 5, o - 1)
            acc_add(dve, 5, KD - 1)

        def context_level(pool, n, l):
            lv = 1 << l
            lef = XL[:, 0:1, T:].rearrange("p d (b t) -> p d b t", t=2 * lv)[:, :, :, 0:lv]
            rig = XR[:, 1:2, T:].rearrange("p d (b t) -> p d b t", t=2 * lv)[:, :, :, lv:2 * lv]
            if l:
                pool.wait_ge(h_xc, at(2 * l, n, 2 * NL + 2))
            pool.tensor_tensor(lef, lef, spread(blocks_of(l, T, TC, 1)[:, 0:1], lv), ALU.mult).then_inc(h_xc, 1)
            pool.tensor_tensor(rig, rig, spread(blocks_of(l, T, TC, 0)[:, 1:2], lv), ALU.mult).then_inc(h_xc, 1)

        def step_pool(pool, n):
            for l in range(NL):
                lv = 1 << l
                if l:
                    pool.wait_ge(h_f, at(l, n, NL))
                    pool.wait_ge(h_xr, at(l, n, NL))
                else:
                    pool.wait_ge(h_in, at(4, n, 4))
                pool.wait_ge(h_mg, at(3 * l + 3, n, 3 * NL))
                right = halves(XR[:, :, 0:T], lv)[1]
                pool.tensor_tensor(right, right, spread(blocks_of(l, 0, T, 0), lv), ALU.mult).then_inc(h_xr, 1)
                context_level(pool, n, l)
            pool.wait_ge(h_f, at(NL, n, NL))
            context_level(pool, n, NL)

        def hg_pool(pool):
            pool.wait_ge(rs_step, 8)
            pool.dma_start(cin[:, :, :], ctxd.rearrange("(a p) d -> p a d", p=P)).then_inc(s_ctx, 16)
            pool.dma_start(mask32[:, :, :], maskd).then_inc(s_mask, 16)
            with pool.Fori(0, HG) as n:
                step_pool(pool, n)

        with ExitStack() as ph:
            tcH = sb("tcH", [P, 2, T], F32R, ph)
            tcL = sb("tcL", [P, 2, T], F32R, ph)
            tsH = sb("tsH", [P, 8, T], F32R, ph)
            tsL = sb("tsL", [P, 8, T], F32R, ph)
            traw = sb("traw", [P, 10, T], F32, ph)
            uH = sb("uH", [P, 2, T], F32R, ph)
            uL = sb("uL", [P, 2, T], F32R, ph)
            fz = sb("fz", [P, 2, T], F32, ph)
            aH = sb("aH", [P, 4, T], F32R, ph)
            aL = sb("aL", [P, 4, T], F32R, ph)
            fy = sb("fy", [P, 2, T], F32, ph)
            fyH = sb("fyH", [P, 2, T], F32R, ph)
            fyL = sb("fyL", [P, 2, T], F32R, ph)

        s_ft = sem("s_ft")
        ft_th = sem("ft_th")
        ft_tl = sem("ft_tl")
        fu_h = sem("fu_h")
        fu_l = sem("fu_l")
        fz_done = sem("fz_done")
        f1 = sem("f1")
        fa_h = sem("fa_h")
        fa_l = sem("fa_l")
        f2 = sem("f2")
        fy_m = sem("fy_m")
        fy_h = sem("fy_h")
        fy_l = sem("fy_l")
        fo = sem("fo")
        xf_done = sem("xf_done")

        FT_R = HG_R + 8 * HG

        def ft_in_pe(pe, s, i, first=None):
            for u in range(4):
                gemm(pe, ps[:, u, :], s + u, i, 6, hH, hL, first if u == 0 else None).then_inc(slot_done, 1)

        def ft_channels_pe(pe, i):
            pe.wait_ge(fu_l, at(2, i, 2))
            pe.wait_ge(fy_m, at(0, i, 2)) if not isinstance(i, int) or i else None
            for t in range(4):
                r = slice(t * P, (t + 1) * P)
                for c in range(2):
                    last = products(pe, ps[:, 4 + t, :], uH[:, c, r], uL[:, c, r], tcH[:, c, :], tcL[:, c, :], c == 0, c == 1)
                last.then_inc(f1, 1)

        def ft_tokens_pe(pe, i):
            pe.wait_ge(fa_l, at(4, i, 4))
            for c in range(2):
                for k in range(8):
                    w = slice(256 * (k // 4) + c * P, 256 * (k // 4) + (c + 1) * P)
                    last = products(pe, ps[:, 4 + c, :], aH[:, k % 4, w], aL[:, k % 4, w], tsH[:, k, :], tsL[:, k, :], k == 0, k == 7)
                last.then_inc(f2, 1)

        def ft_out_pe(pe, s, i, g):
            slot_ready(pe, s + 1, i, 6)
            pe.wait_ge(fy_l, at(2, g, 2))
            pe.wait_ge(fz_done, at(4, g, 2)) if not isinstance(g, int) or g < FG - 1 else None
            for o in range(KD):
                if o >= 4:
                    pe.wait_ge(resid, at(FT_R + o - 3, g, 8))
                w = slice(o * P, (o + 1) * P)
                for c in range(2):
                    j = (s + c) % RING
                    last = products(pe, ps[:, o % 4, :], wh[:, j, w], wl[:, j, w], fyH[:, c, :], fyL[:, c, :], c == 0, c == 1)
                last.then_inc(fo, 1)
            pe.drain().then_inc(slot_done, 2)

        def ft_pe(pe):
            norm_pe(pe, 5, 0)
            ft_in_pe(pe, S_FT, 0, 40)
            pe.wait_ge(ft_tl, 1)
            ft_channels_pe(pe, 0)
            pe.wait_ge(ft_tl, 5)
            ft_tokens_pe(pe, 0)
            ft_in_pe(pe, S_FT + 4, 0)
            with pe.Fori(1, FG - 1) as i:
                ft_channels_pe(pe, i)
                ft_out_pe(pe, S_FT + 2, i, i - 1)
                ft_tokens_pe(pe, i)
                pe.wait_ge(resid, i * 8 + FT_R)
                ft_in_pe(pe, S_FT + 4, i)
            last = FG - 1
            ft_channels_pe(pe, last)
            ft_out_pe(pe, S_FT + 2 + 6 * last, 0, last - 1)
            ft_tokens_pe(pe, last)
            pe.wait_ge(resid, FT_R + 8 * last)
            ft_out_pe(pe, S_FT + 4 + 6 * last, 0, last)

        def ft_in_act(act, s, i, n, between=None):
            for u in range(2):
                split_hi(act, s + u + LEAD, i, 6)
                if between:
                    between(u)
                wait_slot(act, s + u, i, 6)
                act.wait_ge(f1, n * 4) if not isinstance(n, int) or n else None
                act.activation(uH[:, u, :], ps[:, u, :], ACT.Copy).then_inc(fu_h, 1)
            for u in range(2):
                split_hi(act, s + 2 + u + LEAD, i, 6)
                if between:
                    between(2 + u)
                wait_slot(act, s + 2 + u, i, 6)
                act.wait_ge(fy_m, n * 2) if not isinstance(n, int) or n else None
                act.activation(fz[:, u, :], ps[:, 2 + u, :], ACT.Silu).then_inc(fz_done, 1)

        def ft_channels_act(act, i):
            for t in range(4):
                act.wait_ge(f1, at(t + 1, i, 4))
                if t == 0:
                    act.wait_ge(f2, i * 2) if not isinstance(i, int) or i else None
                act.activation(aH[:, t, :], ps[:, 4 + t, :], ACT.Copy).then_inc(fa_h, 1)

        def ft_tokens_act(act, i):
            for c in range(2):
                act.wait_ge(fy_m, at(c + 1, i, 2))
                if c == 0:
                    act.wait_ge(fo, i * 8) if not isinstance(i, int) or i else None
                act.activation(fyH[:, c, :], fy[:, c, :], ACT.Copy).then_inc(fy_h, 1)

        def ft_act(act):
            norm_act(act, 5, 0, mod[:, 96:104])

            def table(n):
                act.wait_ge(s_ft, 16 * (n + 1))
                dst = tcH[:, :, :] if n == 0 else tsH[:, 2 * n - 2:2 * n, :]
                act.activation(dst, traw[:, 2 * n:2 * n + 2, :], ACT.Copy).then_inc(ft_th, 1)

            ft_in_act(act, S_FT, 0, 0, table)
            table(4)
            ft_channels_act(act, 0)
            ft_tokens_act(act, 0)
            ft_in_act(act, S_FT + 4, 0, 1)
            with act.Fori(1, FG - 1) as i:
                split_hi(act, S_FT + 2 + LEAD, i, 6)
                ft_channels_act(act, i)
                split_hi(act, S_FT + 3 + LEAD, i, 6)
                ft_tokens_act(act, i)
                ft_in_act(act, S_FT + 4, i, i + 1)
            last = FG - 1
            s = S_FT + 2 + 6 * last
            split_hi(act, s + LEAD)
            ft_channels_act(act, last)
            split_hi(act, s + 1 + LEAD)
            ft_tokens_act(act, last)
            for o in range(KD):
                act.wait_ge(resid, FT_R + 8 * last + o + 1)
                square(act, 6, o, xT[:, o, :])

        def ft_in_dve(dve, s, i, n, between=None):
            for u in range(2):
                split_lo(dve, s + u + LEAD, i, 6)
                if between:
                    between(u)
                dve.wait_ge(fu_h, at(u + 1, n, 2))
                dve.tensor_tensor(uL[:, u, :], ps[:, u, :], uH[:, u, :].bitcast(F32), ALU.subtract).then_inc(fu_l, 1)
            for u in range(2):
                split_lo(dve, s + 2 + u + LEAD, i, 6)
                if between:
                    between(2 + u)

        def ft_channels_dve(dve, i):
            for t in range(4):
                dve.wait_ge(fa_h, at(t + 1, i, 4))
                dve.tensor_tensor(aL[:, t, :], ps[:, 4 + t, :], aH[:, t, :].bitcast(F32), ALU.subtract).then_inc(fa_l, 1)

        def ft_tokens_dve(dve, i):
            for c in range(2):
                dve.wait_ge(f2, at(c + 1, i, 2))
                dve.wait_ge(fz_done, at(c + 1, i, 2))
                if c == 0:
                    dve.wait_ge(fy_l, i * 2) if not isinstance(i, int) or i else None
                dve.tensor_tensor(fy[:, c, :], ps[:, 4 + c, :], fz[:, c, :], ALU.mult).then_inc(fy_m, 1)
            for c in range(2):
                dve.wait_ge(fy_h, at(c + 1, i, 2))
                dve.tensor_tensor(fyL[:, c, :], fy[:, c, :], fyH[:, c, :].bitcast(F32), ALU.subtract).then_inc(fy_l, 1)

        def ft_out_dve(dve, g, total=False):
            for o in range(KD):
                dve.wait_ge(fo, at(o + 1, g, 8))
                dve.scalar_tensor_tensor(xT[:, o, :], ps[:, o % 4, :], mod[:, 112 + o:113 + o], xT[:, o, :],
                                         ALU.mult, ALU.add).then_inc(resid, 1)
                if total and o:
                    acc_add(dve, 6, o - 1)
            if total:
                acc_add(dve, 6, KD - 1)

        def ft_dve(dve):
            norm_gain(dve, 5, col("norm_g2", 8, 8), mod[:, 104:112])
            norm_dve(dve, 5, mod[:, 96:104])
            acc_clear(dve, 6)

            def table(n):
                dve.wait_ge(ft_th, n + 1)
                hi, lo = (tcH[:, :, :], tcL[:, :, :]) if n == 0 else (tsH[:, 2 * n - 2:2 * n, :], tsL[:, 2 * n - 2:2 * n, :])
                dve.tensor_tensor(lo, traw[:, 2 * n:2 * n + 2, :], hi.bitcast(F32), ALU.subtract).then_inc(ft_tl, 1)

            ft_in_dve(dve, S_FT, 0, 0, table)
            table(4)
            ft_channels_dve(dve, 0)
            ft_tokens_dve(dve, 0)
            ft_in_dve(dve, S_FT + 4, 0, 1)
            with dve.Fori(1, FG - 1) as i:
                split_lo(dve, S_FT + 2 + LEAD, i, 6)
                ft_channels_dve(dve, i)
                ft_out_dve(dve, i - 1)
                split_lo(dve, S_FT + 3 + LEAD, i, 6)
                ft_tokens_dve(dve, i)
                ft_in_dve(dve, S_FT + 4, i, i + 1)
            last = FG - 1
            s = S_FT + 2 + 6 * last
            split_lo(dve, s + LEAD)
            ft_channels_dve(dve, last)
            ft_out_dve(dve, last - 1)
            split_lo(dve, s + 1 + LEAD)
            ft_tokens_dve(dve, last)
            ft_out_dve(dve, last, total=True)

        def ft_pool(pool):
            pool.wait_ge(resid, FT_R)
            for n in range(5):
                src = dftcd if n == 0 else dftsd[:, 2 * n - 2:2 * n, :]
                if n:
                    pool.wait_ge(s_ft, 16 * n)
                pool.dma_start(traw[:, 2 * n:2 * n + 2, :], src).then_inc(s_ft, 16)

        def final_act(act):
            act.preload_act_table_set(EXP_LN)
            act.wait_ge(ms_done, 7)
            act.activation(rs[:, :], ps[:, 4, :], ACT.Ln, bias=epsc[:, :], scale=1.0 / D).then_inc(rs_step, 1)
            act.wait_ge(rs_step, 13)
            act.activation(rs[:, :], rs[:, :], ACT.Exp, scale=-0.5).then_inc(rs_step, 1)

        def final_dve(dve):
            dve.wait_ge(rs_step, 14)
            for k in range(KD):
                dve.scalar_tensor_tensor(xT[:, k, :], xT[:, k, :], col("final_g", k), rs[:, :], ALU.mult, ALU.mult).then_inc(xf_done, 1)

        def finish_pe(pe):
            for k in range(KD):
                src_ready(pe, k)
                for a in range(4):
                    last = pe.transpose(ps[:, (5, 6)[k % 2], a * P:(a + 1) * P], xT[:, k, a * P:(a + 1) * P], const("ident"))
                last.then_inc(fin_t, 1)

        def src_ready(pe, k):
            if k >= 2:
                pe.wait_ge(fin_c, k - 1)
            pe.wait_ge(xf_done, k + 1)

        def finish_act(act):
            for k in range(KD):
                act.wait_ge(fin_t, k + 1)
                act.activation(xout[:, :, k * P:(k + 1) * P], ps[:, (5, 6)[k % 2], :].rearrange("p (a f) -> p a f", a=4),
                               ACT.Copy).then_inc(fin_c, 1)

        with ExitStack() as ph:
            xout = sb("xout", [P, 4, D], F32, ph)

        block = ctx.enter_context(nc.Block())

        @block.sync
        def _(sp):
            sp.dma_start(cols[:, :], colsd).then_inc(s_small, 16)
            sp.dma_start(cst[:, :, :], constd).then_inc(s_small, 16)
            sp.dma_start(xin[:, :, :], xd.rearrange("(a p) d -> p a d", p=P)).then_inc(s_x, 16)
            for u in range(8):
                sp.dma_start(praw[:, u, :], ada[u]).then_inc(s_praw[u], 16)
            for u in range(8):
                sp.wait_ge(s_pacc, u + 1)
                sp.dma_start(praw[:, u, :], ada[8 + u]).then_inc(s_praw[u], 16)
                if u < RING:
                    sp.dma_start(raw[:, u, :], ws[u]).then_inc(loaded[u], 16)
            stream = ws[0:N_SLOTS // RING * RING].rearrange("(g j) p n -> g j p n", j=RING)
            with sp.Fori(1, N_SLOTS // RING) as g:
                for j in range(RING):
                    sp.wait_ge(lo_ready, 3 * g + j + 1)
                    sp.dma_start(raw[:, j, :], stream[bass.ds(g, 1), j].rearrange("a p n -> (a p) n")).then_inc(loaded[j], 16)
            for n in range(N_SLOTS // RING * RING, N_SLOTS):
                sp.wait_ge(lo_ready, n + 1)
                sp.dma_start(raw[:, n % RING, :], ws[n]).then_inc(loaded[n % RING], 16)
            sp.wait_ge(fin_c, 8)
            sp.dma_start(out.rearrange("(a p) d -> p a d", p=P), xout[:, :, :]).then_inc(s_out, 16)
            sp.wait_ge(s_out, 16)

        @block.gpsimd
        def _(pool):
            pool.memset(epsc[:, :], EPS).then_inc(setup, 1)
            pool.wait_ge(s_cact, 1)
            pool.wait_ge(rs_step, 2)
            pool.wait_ge(gain_done, 1)
            with pool.Fori(0, 7) as j:
                ada_load(pool, j, j, ada[16:72])
            mix_pool(pool)
            pool.wait_ge(rs_step, 6)
            pool.wait_ge(gain_done, 3)
            with pool.Fori(7, 13) as j:
                ada_load(pool, j, j - 7, ada[72:120])
            for j in range(2):
                ada_load(pool, 13 + j, j, ada[72:120])
            hg_pool(pool)
            ft_pool(pool)

        @block.scalar
        def _(act):
            act.wait_ge(s_small, 32)
            act.activation(cact[:, :], col("c", 0, 24), ACT.Silu).then_inc(s_cact, 1)
            act.wait_ge(setup, 1)
            for k in range(KD):
                act.wait_ge(xt_t, k + 1)
                act.activation(xT[:, k, :], ps[:, k % 4, :], ACT.Copy).then_inc(xt_c, 1)
                act.wait_ge(acc_step, k + 1)
                act.activation(sq[:, :], ps[:, k % 4, :], ACT.Square).then_inc(sq_done, 1)
            for n in range(LEAD):
                split_hi(act, n)
            norm_act(act, 0, 4, mod[:, 0:8])
            ffn_act(act, 0, S_FFN1, 0)
            mix_act(act)
            norm_act(act, 2, 0, mod[:, 48:56])
            ffn_act(act, 1, S_FFN2, 2)
            hg_act(act)
            ft_act(act)
            final_act(act)
            finish_act(act)

        @block.tensor
        def _(pe):
            pe.sem_inc(slot_done, RING)
            pe.wait_ge(s_x, 16)
            pe.wait_ge(s_small, 32)
            for k in range(KD):
                if k >= 4:
                    pe.wait_ge(sq_done, k - 3)
                for a in range(4):
                    last = pe.transpose(ps[:, k % 4, a * P:(a + 1) * P], xin[:, a, k * P:(k + 1) * P], const("ident"))
                last.then_inc(xt_t, 1)
            norm_pe(pe, 0, 4)
            for v in range(2):
                pe.wait_ge(s_pacc, 8 * v + 8)
                if v:
                    pe.wait_ge(ada_r, 2)
                for j in range(KD):
                    last = pe.transpose(ps[:, 6 + j // 4, (j % 4) * P:(j % 4 + 1) * P], pacc[:, v, j * P:(j + 1) * P], const("ident"))
                last.then_inc(ada_t, 1)
            ffn_pe(pe, 0, S_FFN1, 0)
            mix_pe(pe)
            norm_pe(pe, 2, 0)
            ffn_pe(pe, 1, S_FFN2, 2)
            hg_pe(pe)
            ft_pe(pe)
            norm_pe(pe, 6, 4)
            finish_pe(pe)

        @block.vector
        def _(dve):
            dve.sem_inc(lo_ready, RING)
            dve.sem_inc(h_ms, 1)
            dve.sem_inc(ada_step, ADA_RING)
            dve.sem_inc(ffn_mul, 3)
            dve.sem_inc(ffn_l, 1)
            dve.sem_inc(resid, 2)
            dve.sem_inc(cv_step, 1)
            dve.sem_inc(gb_m, 6)
            dve.sem_inc(gb_l, 1)
            acc_clear(dve, 0)
            dve.wait_ge(s_cact, 1)
            for u in range(16):
                dve.wait_ge(s_praw[u % 8], 16 * (u // 8 + 1))
                if u % 8 == 0:
                    dve.tensor_scalar(pacc[:, u // 8, :], praw[:, 0, :], cact[:, 0:1], None, ALU.mult).then_inc(s_pacc, 1)
                else:
                    dve.wait_ge(s_pacc, u)
                    dve.scalar_tensor_tensor(pacc[:, u // 8, :], praw[:, u % 8, :], cact[:, u % 8:u % 8 + 1],
                                             pacc[:, u // 8, :], ALU.mult, ALU.add).then_inc(s_pacc, 1)
                if u < KD:
                    acc_add(dve, 0, u)
                if u == 11:
                    collect_dve(dve, 0, 0)
            collect_dve(dve, 1, 1)
            for n in range(LEAD):
                split_lo(dve, n)
            dve.wait_ge(ada_r, 6)
            norm_gain(dve, 0, col("norm_w", 0, 8), mod[:, 8:16])
            norm_dve(dve, 0, mod[:, 0:8])
            ffn_dve(dve, 0, S_FFN1, 0)
            mix_dve(dve)
            dve.wait_ge(ada_r, 27)
            norm_gain(dve, 2, col("norm_w", 16, 8), mod[:, 56:64])
            norm_dve(dve, 2, mod[:, 48:56])
            ffn_dve(dve, 1, S_FFN2, 2)
            hg_dve(dve)
            ft_dve(dve)
            final_dve(dve)


def _tiles(w):
    n = w.shape[1] // P
    return w.reshape(-1, P, n, P).transpose(2, 1, 0, 3).reshape(n, P, -1)


def weight_slots(i):
    slots = []

    def ffn(l):
        w13, w2 = i["ffn_w13"][0, l], i["ffn_w2"][0, l]
        g, u = _tiles(w13[:, :FF]), _tiles(w13[:, FF:])
        slots.extend(np.stack([g, u], 1).reshape(2 * KF, P, D))
        pad = np.zeros((W2S * 8 * P, D), w2.dtype)
        pad[:FF] = w2
        slots.extend(pad.reshape(W2S, 8, P, KD, P).transpose(3, 0, 2, 1, 4).reshape(KD * W2S, P, D))

    ffn(0)
    w = i["w_in"][0]
    z32 = np.zeros((D, 32), w.dtype)
    at = QR + KVR
    slots.extend(_tiles(w[:, :at]))
    kr = w[:, at:at + DR]
    slots.extend(_tiles(np.concatenate([kr, z32, kr, z32], 1)))
    at += DR
    conv = _tiles(w[:, at:at + 3 * CW])
    conv = [[conv[t], conv[4 + t], conv[8 + t]] for t in range(4)]
    slots.extend(conv[0])
    at += 3 * CW
    gates = _tiles(w[:, at:])
    uq = i["w_uq"][0].reshape(2, P, HEADS, DN + DR)
    qt = np.zeros((HEADS, 2, P, P), uq.dtype)
    for h in range(HEADS):
        n0, r0 = (0, 64) if h % 2 == 0 else (64, 0)
        qt[h, :, :, n0:n0 + DN] = uq[:, :, h, :DN]
        qt[h, :, :, r0:r0 + DR] = uq[:, :, h, DN:]
    slots.extend(qt.reshape(2, 4, 2, P, P).transpose(0, 3, 1, 2, 4).reshape(2, P, D))
    ukv = i["w_ukv"][0].reshape(P, HEADS, DN + DV)
    slots.append(np.concatenate([ukv[:, :, :DN].reshape(P, -1), ukv[:, :, DN:].reshape(P, -1)], 1))
    for t in range(1, 4):
        slots.extend(conv[t])
    br = _tiles(i["w_branch"][0].reshape(D, D))
    for o in range(KD):
        slots.extend([gates[o], gates[KD + o], br[o]])
    slots.extend(_tiles(i["w_out"][0]))
    ffn(1)
    s5 = _tiles(i["hg_w_in_2"][0]).reshape(5, HG, P, D)
    wo = i["hg_w_out_2"][0].reshape(HG, P, D)
    for h in range(-1, HG):
        if h + 1 < HG:
            slots.extend([s5[1, h + 1], s5[2, h + 1]])
        if h >= 1:
            slots.append(wo[h - 1])
        if h + 1 < HG:
            slots.extend([s5[0, h + 1], s5[4, h + 1], s5[3, h + 1]])
    slots.append(wo[HG - 1])
    fi = _tiles(i["ft_w_in_2"][0])
    fo = i["ft_w_out_2"][0].reshape(2 * FG, P, D)
    for g in range(FG):
        if g >= 2:
            slots.extend([fo[2 * g - 4], fo[2 * g - 3]])
        slots.extend([fi[2 * g], fi[2 * g + 1], fi[16 + 2 * g], fi[17 + 2 * g]])
    slots.extend(fo[2 * FG - 4:])
    return np.ascontiguousarray(np.stack(slots))


def host_arrays(i):
    f = np.float32
    a1 = i["w_ada"][0].reshape(KD, P, 9, D).transpose(2, 0, 1, 3).reshape(72, P, D)
    a2 = i["ada_w_2"].reshape(2, KD, P, 3, D).transpose(0, 3, 1, 2, 4).reshape(48, P, D)
    ada = np.concatenate([a1, a2])

    def c8(v):
        return v.reshape(-1, P).T

    b2 = i["ada_b_2"].reshape(6, D)
    z = np.zeros(32, f)
    qn, qr = i["q_norm_nope"][0], i["q_norm_rope"][0]
    kr = i["k_norm_rope"][0]
    cols = {
        "bias": np.concatenate([c8(i["b_ada"][0]), c8(b2), c8(b2[:2])], 1),
        "c": np.concatenate([c8(i["c"][0]), c8(i["c_2"][0]), c8(i["c_ctx_2"])], 1),
        "norm_w": c8(i["norm_w"][0]), "norm_g2": c8(i["norm_g_2"]), "final_g": c8(i["final_g_2"]),
        "qa": c8(i["q_a_norm"][0]), "kva": c8(i["kv_a_norm"][0]),
        "qe": np.concatenate([qn, qr, z])[:, None], "qo": np.concatenate([qr, z, qn])[:, None],
        "kn": np.concatenate([i["k_norm_nope"][0]] * 2)[:, None], "kr": np.concatenate([kr, z, kr, z])[:, None],
        "conv": i["conv_w"][0].reshape(3, 4, P).transpose(2, 1, 0).reshape(P, 12),
        "hg_norm": i["hg_norm_g_2"][0][:, None],
        "lb": i["hg_lb_logits_2"].reshape(2, 2, HG, P).transpose(3, 0, 1, 2).reshape(P, 64),
        "inv_freq": np.tile(1.0 / (10000.0 ** (np.arange(0, DR, 2, dtype=f) / f(DR))), 8).astype(f)[:, None],
    }
    colsd = np.ascontiguousarray(np.concatenate([cols[n] for n in COLS], 1))
    r = np.arange(P)

    def blocks(sizes):
        m, a = np.zeros((P, P), f), 0
        for n in sizes:
            m[a:a + n, a:a + n] = 1.0 / n
            a += n
        return m

    rot = np.zeros((P, P), f)
    for m in range(P):
        rot[m + 16 if m % 32 < 16 else m - 16, m] = -1.0 if m % 32 < 16 else 1.0
    const = {"ident": np.eye(P, dtype=f), "ones": np.ones((P, P), f), "bd_even": blocks([64, 32, 32]),
             "bd_odd": blocks([32, 32, 64]), "bd_k": blocks([64, 64]), "bd_rope": blocks([32] * 4), "rot": rot,
             "causal": np.where(r[None, :] <= r[:, None], 0.0, NEG).astype(f)}
    constd = np.ascontiguousarray(np.stack([const[n] for n in CONST], 1))
    s, t = r[:, None], r[None, :]
    masks = [s == t] + [(s // (2 * lv) == t // (2 * lv)) & (s // lv != t // lv) for lv in LEVELS]
    maskd = np.ascontiguousarray(np.stack(masks, 1).astype(np.int32))
    d = 256
    a = 2 * np.pi * np.outer(np.arange(d), np.arange(d)) / d
    dftc = np.concatenate([np.cos(a), np.sin(a)], 1).reshape(2, P, 2 * d).transpose(1, 0, 2).astype(f)
    a = 2 * np.pi * np.outer(np.arange(T), np.arange(T)) / T
    n = 1.0 / np.sqrt(T * d)
    dfts = np.concatenate([np.cos(a) * n, -np.sin(a) * n], 0).reshape(8, P, T).transpose(1, 0, 2).astype(f)
    return {"ws": weight_slots(i), "ada": ada, "cols": colsd, "const": constd, "mask": maskd,
            "dftc": np.ascontiguousarray(dftc), "dfts": np.ascontiguousarray(dfts),
            "x": i["x"][0], "ctx": i["ctx_2"][0], "pos": i["positions"]}


def kernel(**inputs):
    import concourse.bacc as _bacc
    from concourse import mybir as _mybir
    from concourse.bass_utils import run_bass_kernel_spmd as _run

    arrays = {k: np.ascontiguousarray(v) for k, v in host_arrays({k: np.asarray(v) for k, v in inputs.items()}).items()}
    nc = _bacc.Bacc("TRN2", target_bir_lowering=False, num_devices=1)
    args = [nc.dram_tensor(f"in_{k}", v.shape, _mybir.dt.from_np(v.dtype), kind="ExternalInput").ap() for k, v in arrays.items()]
    out = nc.dram_tensor("out_x", (T, D), F32, kind="ExternalOutput").ap()
    build(nc, *args, out)
    r = _run(nc, [{f"in_{k}": v for k, v in arrays.items()}], core_ids=[0])
    return r.results[0]["out_x"].reshape(1, T, D)
```
